# Optimizing a Trainium2 kernel written in Bass

```python
import jax, jax.numpy as jnp
from jax import lax
import numpy as np
import math

D_MODEL = 1024
BATCH = 1
SEQ = 512
DEPTH = 2

GRID_W = 64
CTX_LEN = 256
HEAD_DIM = 64
ROPE_THETA = 10000.0
Q_BLOCK = 128
RMS_EPS = 1e-6
H_A = 8
NOPE_A = 64
ROPE_A = 32
V_A = 64
Q_LORA = 384
KV_LORA = 256
H_B = 8
KV_B = 2
G_B = H_B // KV_B
AB_IN = Q_LORA + KV_LORA + ROPE_A + H_B * HEAD_DIM + 2 * KV_B * HEAD_DIM
AB_OUT = H_A * V_A + H_B * HEAD_DIM
H_C = 16
WIN_R = 8
WIN_C = 16
C_WIDTH = H_C * HEAD_DIM
N_GROUPS = 4
EXPERTS_PER_GROUP = 8
N_EXPERTS = N_GROUPS * EXPERTS_PER_GROUP
TOP_K = 2
D_EXPERT = 512
MOE_BLOCK = 128
N_EVEN = (DEPTH + 1) // 2
N_ODD = DEPTH // 2


def rmsnorm(x, g):
    xf = x.astype(jnp.float32)
    y = xf * lax.rsqrt(jnp.mean(xf * xf, axis=-1, keepdims=True) + RMS_EPS)
    return (y * g.astype(jnp.float32)).astype(x.dtype)

def modulate(x, g, shift, scale):
    return rmsnorm(x, g) * (1 + scale) + shift

def axial_rope_table(rows, cols, rot_dim):
    n = rot_dim // 4
    inv = ROPE_THETA ** (-jnp.arange(n, dtype=jnp.float32) / n)
    ang = jnp.concatenate([rows[:, None] * inv, cols[:, None] * inv], axis=-1)
    return jnp.cos(ang), jnp.sin(ang)

def apply_rope(x, rope):
    cos, sin = rope
    cos = cos.astype(x.dtype)
    sin = sin.astype(x.dtype)
    x1 = x[..., 0::2]
    x2 = x[..., 1::2]
    return jnp.stack([x1 * cos - x2 * sin, x1 * sin + x2 * cos], axis=-1).reshape(x.shape)

def heads_to_tokens(o):
    b, h, t, d = o.shape
    return o.transpose(0, 2, 1, 3).reshape(b, t, h * d)

def attend(q, k, v):
    s = jnp.einsum('bhgqd,bhkd->bhgqk', q, k, preferred_element_type=jnp.float32)
    p = jax.nn.softmax(s, axis=-1).astype(v.dtype)
    return jnp.einsum('bhgqk,bhkd->bhgqd', p, v)

def prefix_attention(q, k_lat, v_lat, k_ctx, v_ctx):
    b, hk, g, s, d = q.shape
    nb = s // Q_BLOCK
    k_all = jnp.concatenate([k_ctx, k_lat], axis=2)
    v_all = jnp.concatenate([v_ctx, v_lat], axis=2)
    qb = q.reshape(b, hk, g, nb, Q_BLOCK, d).transpose(3, 0, 1, 2, 4, 5)
    o = lax.map(lambda qblk: attend(qblk, k_all, v_all), qb)
    return o.transpose(1, 2, 3, 0, 4, 5).reshape(b, hk, g, s, v_all.shape[-1])

def mixer_ab(h_ctx, h_lat, rope_a, rope_b, w_in, w_out, q_norm, w_q_up, kv_norm, w_kv_up, gq_norm, gk_norm, need_ctx):
    def project(h, ra, rb):
        bsz, t, _ = h.shape
        p = h @ w_in
        o0 = Q_LORA
        o1 = o0 + KV_LORA
        o2 = o1 + ROPE_A
        o3 = o2 + H_B * HEAD_DIM
        o4 = o3 + KV_B * HEAD_DIM
        cq, ckv, kr = p[..., :o0], p[..., o0:o1], p[..., o1:o2]
        gq, gk, gv = p[..., o2:o3], p[..., o3:o4], p[..., o4:]
        qa = (rmsnorm(cq, q_norm) @ w_q_up).reshape(bsz, t, H_A, NOPE_A + ROPE_A).transpose(0, 2, 1, 3)
        kva = (rmsnorm(ckv, kv_norm) @ w_kv_up).reshape(bsz, t, H_A, NOPE_A + V_A).transpose(0, 2, 1, 3)
        q_nope, q_rope = qa[..., :NOPE_A], qa[..., NOPE_A:]
        k_nope, va = kva[..., :NOPE_A], kva[..., NOPE_A:]
        k_rope = kr[:, None]
        if ra is not None:
            q_rope = apply_rope(q_rope, ra)
            k_rope = apply_rope(k_rope, ra)
        qa = jnp.concatenate([q_nope, q_rope], axis=-1) * ((NOPE_A + ROPE_A) ** -0.5)
        ka = jnp.concatenate([k_nope, jnp.broadcast_to(k_rope, (bsz, H_A, t, ROPE_A))], axis=-1)
        qb = rmsnorm(gq.reshape(bsz, t, H_B, HEAD_DIM).transpose(0, 2, 1, 3), gq_norm)
        kb = rmsnorm(gk.reshape(bsz, t, KV_B, HEAD_DIM).transpose(0, 2, 1, 3), gk_norm)
        vb = gv.reshape(bsz, t, KV_B, HEAD_DIM).transpose(0, 2, 1, 3)
        if rb is not None:
            qb = apply_rope(qb, rb)
            kb = apply_rope(kb, rb)
        qb = qb.reshape(bsz, KV_B, G_B, t, HEAD_DIM) * (HEAD_DIM ** -0.5)
        return qa[:, :, None], ka, va, qb, kb, vb

    qa_l, ka_l, va_l, qb_l, kb_l, vb_l = project(h_lat, rope_a, rope_b)
    qa_c, ka_c, va_c, qb_c, kb_c, vb_c = project(h_ctx, None, None)
    bsz, s = h_lat.shape[0], h_lat.shape[1]
    oa = prefix_attention(qa_l, ka_l, va_l, ka_c, va_c).reshape(bsz, H_A, s, V_A)
    ob = prefix_attention(qb_l, kb_l, vb_l, kb_c, vb_c).reshape(bsz, H_B, s, HEAD_DIM)
    out_lat = jnp.concatenate([heads_to_tokens(oa), heads_to_tokens(ob)], axis=-1) @ w_out
    out_ctx = None
    if need_ctx:
        t = h_ctx.shape[1]
        oa_c = attend(qa_c, ka_c, va_c).reshape(bsz, H_A, t, V_A)
        ob_c = attend(qb_c, kb_c, vb_c).reshape(bsz, H_B, t, HEAD_DIM)
        out_ctx = jnp.concatenate([heads_to_tokens(oa_c), heads_to_tokens(ob_c)], axis=-1) @ w_out
    return out_ctx, out_lat

def mixer_na(h_ctx, h_lat, nbr_idx, rel_idx, w_in, w_out, rpb, need_ctx):
    def project(h):
        bsz, t, _ = h.shape
        p = (h @ w_in).reshape(bsz, t, 3, H_C, HEAD_DIM).transpose(2, 0, 3, 1, 4)
        return p[0] * (HEAD_DIM ** -0.5), p[1], p[2]

    q_l, k_l, v_l = project(h_lat)
    q_c, k_c, v_c = project(h_ctx)
    bsz, s = h_lat.shape[0], h_lat.shape[1]
    nk = nbr_idx.shape[1]
    nb = s // Q_BLOCK
    rpb_flat = rpb.reshape(H_C, -1)
    qb = q_l.reshape(bsz, H_C, nb, Q_BLOCK, HEAD_DIM).transpose(2, 0, 1, 3, 4)
    idx_b = nbr_idx.reshape(nb, Q_BLOCK, nk)
    rel_b = rel_idx.reshape(nb, Q_BLOCK, nk)

    def one_block(args):
        qblk, ib, rb = args
        kg = jnp.take(k_l, ib, axis=2)
        vg = jnp.take(v_l, ib, axis=2)
        s_n = jnp.einsum('bhqd,bhqnd->bhqn', qblk, kg, preferred_element_type=jnp.float32) + rpb_flat[:, rb].astype(jnp.float32)
        s_c = jnp.einsum('bhqd,bhcd->bhqc', qblk, k_c, preferred_element_type=jnp.float32)
        p = jax.nn.softmax(jnp.concatenate([s_n, s_c], axis=-1), axis=-1).astype(v_l.dtype)
        return jnp.einsum('bhqn,bhqnd->bhqd', p[..., :nk], vg) + jnp.einsum('bhqc,bhcd->bhqd', p[..., nk:], v_c)

    o = lax.map(one_block, (qb, idx_b, rel_b))
    out_lat = o.transpose(1, 0, 3, 2, 4).reshape(bsz, s, C_WIDTH) @ w_out
    out_ctx = None
    if need_ctx:
        oc = attend(q_c[:, :, None], k_c, v_c)[:, :, 0]
        out_ctx = heads_to_tokens(oc) @ w_out
    return out_ctx, out_lat

def hier_moe(h, w_rg, b_rg, w_re, b_re, w_gate, w_up, w_down):
    n, d = h.shape
    hf = h.astype(jnp.float32)
    pg = jax.nn.softmax(hf @ w_rg.astype(jnp.float32) + b_rg.astype(jnp.float32), axis=-1)
    g_sel = jnp.argmax(pg, axis=-1)
    p_gsel = jnp.take_along_axis(pg, g_sel[:, None], axis=-1)
    le = (hf @ w_re.astype(jnp.float32) + b_re.astype(jnp.float32)).reshape(n, N_GROUPS, EXPERTS_PER_GROUP)
    le_sel = jnp.take_along_axis(le, g_sel[:, None, None], axis=1)[:, 0]
    top_p, top_i = lax.top_k(jax.nn.softmax(le_sel, axis=-1), TOP_K)
    gate_w = p_gsel * top_p / jnp.sum(top_p, axis=-1, keepdims=True)
    experts = g_sel[:, None] * EXPERTS_PER_GROUP + top_i

    nkk = n * TOP_K
    flat_e = experts.reshape(-1).astype(jnp.int32)
    flat_w = gate_w.reshape(-1)
    order = jnp.argsort(flat_e)
    sorted_e = flat_e[order]
    tok_sorted = (jnp.arange(nkk, dtype=jnp.int32) // TOP_K)[order]
    w_sorted = flat_w[order]
    counts = jnp.bincount(flat_e, length=N_EXPERTS)
    padded = ((counts + MOE_BLOCK - 1) // MOE_BLOCK) * MOE_BLOCK
    ends = jnp.cumsum(padded)
    pad_start = ends - padded
    start = jnp.cumsum(counts) - counts
    rank = jnp.arange(nkk, dtype=jnp.int32) - start[sorted_e]
    dest = pad_start[sorted_e] + rank
    total = -(-(nkk + N_EXPERTS * (MOE_BLOCK - 1)) // MOE_BLOCK) * MOE_BLOCK
    nblk = total // MOE_BLOCK
    buf_tok = jnp.full((total,), n, jnp.int32).at[dest].set(tok_sorted)
    h_pad = jnp.concatenate([h, jnp.zeros((1, d), h.dtype)], axis=0)
    x_buf = h_pad[buf_tok].reshape(nblk, MOE_BLOCK, d)
    blk_e = jnp.clip(jnp.searchsorted(ends, jnp.arange(nblk, dtype=ends.dtype) * MOE_BLOCK, side='right'), 0, N_EXPERTS - 1)

    def run_block(args):
        xb, e = args
        return (jax.nn.silu(xb @ w_gate[e]) * (xb @ w_up[e])) @ w_down[e]

    y = lax.map(run_block, (x_buf, blk_e)).reshape(total, d)
    return jnp.zeros((n, d), h.dtype).at[tok_sorted].add(y[dest] * w_sorted[:, None].astype(h.dtype))

def first_inputs(seed: int = 0) -> dict:
    key = jax.random.key(seed)
    ks = jax.random.split(key, 32)

    def nrm(k, shape, scale):
        return jax.random.normal(k, shape, jnp.float32) * scale

    def gain(k, shape):
        return 1.0 + nrm(k, shape, 0.1)

    D = D_MODEL
    return {
        "x": nrm(ks[0], (BATCH, SEQ, D), 1.0),
        "c": nrm(ks[1], (BATCH, D), 1.0),
        "ctx": nrm(ks[2], (BATCH, CTX_LEN, D), 1.0),
        "c_ctx": nrm(ks[3], (D,), 1.0),
        "w_ada": nrm(ks[4], (DEPTH, D, 6 * D), 0.02),
        "b_ada": nrm(ks[5], (DEPTH, 6 * D), 0.02),
        "norm_mix": gain(ks[6], (DEPTH, D)),
        "norm_ffn": gain(ks[7], (DEPTH, D)),
        "norm_final": gain(ks[8], (D,)),
        "ab_w_in": nrm(ks[9], (N_EVEN, D, AB_IN), D ** -0.5),
        "ab_w_out": nrm(ks[10], (N_EVEN, AB_OUT, D), AB_OUT ** -0.5),
        "mla_q_norm": gain(ks[11], (N_EVEN, Q_LORA)),
        "mla_w_q_up": nrm(ks[12], (N_EVEN, Q_LORA, H_A * (NOPE_A + ROPE_A)), Q_LORA ** -0.5),
        "mla_kv_norm": gain(ks[13], (N_EVEN, KV_LORA)),
        "mla_w_kv_up": nrm(ks[14], (N_EVEN, KV_LORA, H_A * (NOPE_A + V_A)), KV_LORA ** -0.5),
        "gqa_q_norm": gain(ks[15], (N_EVEN, HEAD_DIM)),
        "gqa_k_norm": gain(ks[16], (N_EVEN, HEAD_DIM)),
        "na_w_in": nrm(ks[17], (N_ODD, D, 3 * C_WIDTH), D ** -0.5),
        "na_w_out": nrm(ks[18], (N_ODD, C_WIDTH, D), C_WIDTH ** -0.5),
        "na_rpb": nrm(ks[19], (N_ODD, H_C, 2 * WIN_R - 1, 2 * WIN_C - 1), 0.1),
        "moe_w_rg": nrm(ks[20], (DEPTH, D, N_GROUPS), D ** -0.5),
        "moe_b_rg": nrm(ks[21], (DEPTH, N_GROUPS), 0.01),
        "moe_w_re": nrm(ks[22], (DEPTH, D, N_EXPERTS), D ** -0.5),
        "moe_b_re": nrm(ks[23], (DEPTH, N_EXPERTS), 0.01),
        "moe_w_gate": nrm(ks[24], (DEPTH, N_EXPERTS, D, D_EXPERT), D ** -0.5),
        "moe_w_up": nrm(ks[25], (DEPTH, N_EXPERTS, D, D_EXPERT), D ** -0.5),
        "moe_w_down": nrm(ks[26], (DEPTH, N_EXPERTS, D_EXPERT, D), D_EXPERT ** -0.5),
    }

def first_block(x, c, ctx, c_ctx, w_ada, b_ada, norm_mix, norm_ffn, norm_final, ab_w_in, ab_w_out, mla_q_norm, mla_w_q_up, mla_kv_norm, mla_w_kv_up, gqa_q_norm, gqa_k_norm, na_w_in, na_w_out, na_rpb, moe_w_rg, moe_b_rg, moe_w_re, moe_b_re, moe_w_gate, moe_w_up, moe_w_down):
    bsz, s, d = x.shape
    n_ctx = ctx.shape[1]
    rows_n = s // GRID_W
    wr = min(WIN_R, rows_n)
    t = jnp.arange(s, dtype=jnp.int32)
    r = t // GRID_W
    col = t % GRID_W
    rope_a = axial_rope_table(r.astype(jnp.float32), col.astype(jnp.float32), ROPE_A)
    rope_b = axial_rope_table(r.astype(jnp.float32), col.astype(jnp.float32), HEAD_DIM)
    rs = jnp.clip(r - wr // 2, 0, rows_n - wr)
    cs = jnp.clip(col - WIN_C // 2, 0, GRID_W - WIN_C)
    key_r = rs[:, None] + jnp.arange(wr, dtype=jnp.int32)[None]
    key_c = cs[:, None] + jnp.arange(WIN_C, dtype=jnp.int32)[None]
    nbr_idx = (key_r[:, :, None] * GRID_W + key_c[:, None, :]).reshape(s, wr * WIN_C)
    rel_idx = ((key_r - r[:, None] + WIN_R - 1)[:, :, None] * (2 * WIN_C - 1)
               + (key_c - col[:, None] + WIN_C - 1)[:, None, :]).reshape(s, wr * WIN_C)

    x_lat = x
    x_ctx = ctx
    silu_c = jax.nn.silu(c)
    silu_cc = jax.nn.silu(c_ctx)
    for l in range(DEPTH):
        last = l == DEPTH - 1
        mod_l = (silu_c @ w_ada[l] + b_ada[l])[:, None, :]
        mod_c = (silu_cc @ w_ada[l] + b_ada[l])[None, None, :]
        sh1, sc1, g1, sh2, sc2, g2 = jnp.split(mod_l, 6, axis=-1)
        sh1c, sc1c, g1c, sh2c, sc2c, g2c = jnp.split(mod_c, 6, axis=-1)
        h_l = modulate(x_lat, norm_mix[l], sh1, sc1)
        h_c = modulate(x_ctx, norm_mix[l], sh1c, sc1c)
        if l % 2 == 0:
            i = l // 2
            o_c, o_l = mixer_ab(h_c, h_l, rope_a, rope_b, ab_w_in[i], ab_w_out[i], mla_q_norm[i], mla_w_q_up[i],
                                mla_kv_norm[i], mla_w_kv_up[i], gqa_q_norm[i], gqa_k_norm[i], not last)
        else:
            i = l // 2
            o_c, o_l = mixer_na(h_c, h_l, nbr_idx, rel_idx, na_w_in[i], na_w_out[i], na_rpb[i], not last)
        x_lat = x_lat + g1 * o_l
        h_l = modulate(x_lat, norm_ffn[l], sh2, sc2)
        if not last:
            x_ctx = x_ctx + g1c * o_c
            h_c = modulate(x_ctx, norm_ffn[l], sh2c, sc2c)
            tokens = jnp.concatenate([h_c.reshape(-1, d), h_l.reshape(-1, d)], axis=0)
            y = hier_moe(tokens, moe_w_rg[l], moe_b_rg[l], moe_w_re[l], moe_b_re[l], moe_w_gate[l], moe_w_up[l], moe_w_down[l])
            n_c = bsz * n_ctx
            x_ctx = x_ctx + g2c * y[:n_c].reshape(bsz, n_ctx, d)
            x_lat = x_lat + g2 * y[n_c:].reshape(bsz, s, d)
        else:
            y = hier_moe(h_l.reshape(-1, d), moe_w_rg[l], moe_b_rg[l], moe_w_re[l], moe_b_re[l], moe_w_gate[l], moe_w_up[l], moe_w_down[l])
            x_lat = x_lat + g2 * y.reshape(bsz, s, d)
    return rmsnorm(x_lat, norm_final)


RET_HEADS = 4
RET_HEAD_DIM = 128
RET_CHUNK = 128
DSA_HEADS = 8
DSA_HEAD_DIM = 64
DSA_PATTERNS = ((128, 1), (512, 4), (2048, 16))
DSA_BLOCK = 128
T5_BUCKETS = 32
T5_MAX_DIST = 2048
MLSTM_HEADS = 4
MLSTM_HEAD_DIM = 256
MLSTM_CHUNK = 128
MLSTM_CONV = 4
D_FF = 2816
FFN_CONV = 3
LN_EPS = 1e-5
DEEPNORM_ALPHA = (2.0 * DEPTH) ** 0.25
DEEPNORM_BETA = (8.0 * DEPTH) ** -0.25

N_EVEN_2 = (DEPTH + 1) // 2
N_ODD_2 = DEPTH // 2
RET_W = RET_HEADS * RET_HEAD_DIM
DSA_W = DSA_HEADS * DSA_HEAD_DIM
MIX_W_EVEN = RET_W + DSA_W
EVEN_IN = 4 * RET_W + 3 * DSA_W
EVEN_SPLITS = (RET_W, 2 * RET_W, 3 * RET_W, 4 * RET_W, 4 * RET_W + DSA_W, 4 * RET_W + 2 * DSA_W)
MLSTM_W = MLSTM_HEADS * MLSTM_HEAD_DIM
ODD_IN = 4 * MLSTM_W + 2 * MLSTM_HEADS
ODD_SPLITS = (2 * MLSTM_W, 3 * MLSTM_W, 4 * MLSTM_W)


def layer_norm(x, g, b):
    xf = x.astype(jnp.float32)
    mu = jnp.mean(xf, -1, keepdims=True)
    var = jnp.mean(jnp.square(xf - mu), -1, keepdims=True)
    return ((xf - mu) * lax.rsqrt(var + LN_EPS) * g + b).astype(x.dtype)

def head_norm(y):
    mu = jnp.mean(y, -1, keepdims=True)
    var = jnp.mean(jnp.square(y - mu), -1, keepdims=True)
    return (y - mu) * lax.rsqrt(var + LN_EPS)

def split_heads(t, n_heads):
    B, S, W = t.shape
    return t.reshape(B, S, n_heads, W // n_heads).transpose(0, 2, 1, 3)

def merge_heads(t):
    B, H, S, d = t.shape
    return t.transpose(0, 2, 1, 3).reshape(B, S, H * d)

def causal_dwconv(x, w):
    K, C = w.shape
    return lax.conv_general_dilated(x, w[:, None, :].astype(x.dtype), window_strides=(1,), padding=[(K - 1, 0)], dimension_numbers=("NWC", "WIO", "NWC"), feature_group_count=C)

def rotary(x):
    S, d = x.shape[-2], x.shape[-1]
    inv = 1.0 / (10000.0 ** (jnp.arange(0, d, 2, dtype=jnp.float32) / d))
    ang = jnp.arange(S, dtype=jnp.float32)[:, None] * inv[None, :]
    cos, sin = jnp.cos(ang), jnp.sin(ang)
    x1, x2 = x[..., : d // 2], x[..., d // 2:]
    return jnp.concatenate([x1 * cos - x2 * sin, x1 * sin + x2 * cos], -1)

def retention(q, k, v):
    B, H, S, d = q.shape
    C = RET_CHUNK
    N = S // C
    log_gamma = jnp.log1p(-jnp.exp2(-5.0 - jnp.arange(H, dtype=jnp.float32)))
    qf = rotary(q.astype(jnp.float32))
    kf = rotary(k.astype(jnp.float32)) * (d ** -0.5)
    qc = qf.reshape(B, H, N, C, d)
    kc = kf.reshape(B, H, N, C, d)
    vc = v.astype(jnp.float32).reshape(B, H, N, C, d)
    idx = jnp.arange(C, dtype=jnp.float32)
    rel = idx[:, None] - idx[None, :]
    decay = jnp.where(rel >= 0, jnp.exp(log_gamma[:, None, None] * jnp.maximum(rel, 0.0)), 0.0)
    scores = jnp.einsum('bhncd,bhnsd->bhncs', qc, kc) * decay[None, :, None]
    y_intra = jnp.einsum('bhncs,bhnse->bhnce', scores, vc)
    k_w = jnp.exp(log_gamma[:, None] * (C - 1 - idx)[None, :])
    kv = jnp.einsum('bhnsd,bhnse->bhnde', kc * k_w[None, :, None, :, None], vc)
    chunk_decay = jnp.exp(log_gamma * C)[None, :, None, None]

    def step(R, kv_n):
        return chunk_decay * R + kv_n, R

    _, R_prev = lax.scan(step, jnp.zeros((B, H, d, d), jnp.float32), jnp.moveaxis(kv, 2, 0))
    R_prev = jnp.moveaxis(R_prev, 0, 2)
    q_w = jnp.exp(log_gamma[:, None] * (idx + 1.0)[None, :])
    y_inter = jnp.einsum('bhncd,bhnde->bhnce', qc * q_w[None, :, None, :, None], R_prev)
    return (y_intra + y_inter).reshape(B, H, S, d)

def t5_bucket(dist):
    exact = T5_BUCKETS // 2
    n = jnp.maximum(dist, 0)
    large = exact + (jnp.log(jnp.maximum(n, 1).astype(jnp.float32) / exact) / math.log(T5_MAX_DIST / exact) * (T5_BUCKETS - exact)).astype(jnp.int32)
    large = jnp.minimum(large, T5_BUCKETS - 1)
    return jnp.where(n < exact, n, large)

def dilated_branch(q, k, v, rel_bias, window, dilation):
    B, H, S, d = q.shape
    L = S // dilation
    W = window // dilation
    blk = DSA_BLOCK
    nb = -(-L // blk)
    Lp = nb * blk

    def to_blocks(t):
        t = t.astype(jnp.float32).reshape(B, H, L, dilation, d).swapaxes(2, 3)
        t = jnp.pad(t, ((0, 0), (0, 0), (0, 0), (0, Lp - L), (0, 0)))
        return t.reshape(B, H, dilation, nb, blk, d)

    def with_prev(t):
        prev = jnp.pad(t[:, :, :, :-1], ((0, 0), (0, 0), (0, 0), (1, 0), (0, 0), (0, 0)))
        return jnp.concatenate([prev, t], axis=4)

    qb = to_blocks(q)
    kw = with_prev(to_blocks(k))
    vw = with_prev(to_blocks(v))
    qi = jnp.arange(blk)[:, None] + blk
    kj = jnp.arange(2 * blk)[None, :]
    dist = qi - kj
    bias = rel_bias[t5_bucket(dist * dilation)].astype(jnp.float32).transpose(2, 0, 1)
    blk_start = jnp.arange(nb)[:, None, None] * blk
    valid = (dist >= 0) & (dist <= W) & (blk_start + kj - blk >= 0)
    logits = jnp.einsum('bhrnqd,bhrnkd->bhrnqk', qb, kw) * (d ** -0.5) + bias[None, :, None, None]
    logits = jnp.where(valid, logits, -jnp.inf)
    m = jnp.max(logits, -1)
    p = jnp.exp(logits - m[..., None])
    s = jnp.sum(p, -1)
    o = jnp.einsum('bhrnqk,bhrnkd->bhrnqd', p, vw)

    def from_blocks(t):
        tail = t.shape[5:]
        t = t.reshape((B, H, dilation, Lp) + tail)[:, :, :, :L]
        return jnp.swapaxes(t, 2, 3).reshape((B, H, S) + tail)

    return from_blocks(m), from_blocks(s), from_blocks(o)

def dilated_attention(q, k, v, rel_bias):
    outs = [dilated_branch(q, k, v, rel_bias, w, r) for (w, r) in DSA_PATTERNS]
    M = jnp.max(jnp.stack([m for (m, _, _) in outs]), axis=0)
    num = sum(jnp.exp(m - M)[..., None] * o for (m, _, o) in outs)
    den = sum(jnp.exp(m - M) * s for (m, s, _) in outs)
    return num / den[..., None]

def mlstm(q, k, v, log_i, log_f):
    B, H, S, d = q.shape
    C = MLSTM_CHUNK
    N = S // C
    qc = q.astype(jnp.float32).reshape(B, H, N, C, d)
    kc = (k.astype(jnp.float32) * (d ** -0.5)).reshape(B, H, N, C, d)
    vc = v.astype(jnp.float32).reshape(B, H, N, C, d)
    li = log_i.reshape(B, H, N, C)
    a = jnp.cumsum(log_f.reshape(B, H, N, C), axis=-1)
    g = a[..., -1]
    w_state = g[..., None] - a + li
    m_loc = jnp.max(w_state, -1)
    ew = jnp.exp(w_state - m_loc[..., None])[..., None]
    kv = jnp.einsum('bhncd,bhnce->bhnde', kc * ew, vc)
    ksum = jnp.sum(kc * ew, axis=3)

    def step(carry, inp):
        C_s, n_s, m_s = carry
        kv_n, ks_n, g_n, m_n = inp
        m_new = jnp.maximum(g_n + m_s, m_n)
        a_old = jnp.exp(g_n + m_s - m_new)
        a_loc = jnp.exp(m_n - m_new)
        C_new = a_old[..., None, None] * C_s + a_loc[..., None, None] * kv_n
        n_new = a_old[..., None] * n_s + a_loc[..., None] * ks_n
        return (C_new, n_new, m_new), (C_s, n_s, m_s)

    init = (jnp.zeros((B, H, d, d), jnp.float32), jnp.zeros((B, H, d), jnp.float32), jnp.zeros((B, H), jnp.float32))
    xs = (jnp.moveaxis(kv, 2, 0), jnp.moveaxis(ksum, 2, 0), jnp.moveaxis(g, 2, 0), jnp.moveaxis(m_loc, 2, 0))
    _, (C_prev, n_prev, m_prev) = lax.scan(step, init, xs)
    C_prev = jnp.moveaxis(C_prev, 0, 2)
    n_prev = jnp.moveaxis(n_prev, 0, 2)
    m_prev = jnp.moveaxis(m_prev, 0, 2)
    D = a[..., :, None] - a[..., None, :] + li[..., None, :]
    causal = jnp.tril(jnp.ones((C, C), dtype=bool))
    D = jnp.where(causal, D, -jnp.inf)
    inter_log = a + m_prev[..., None]
    m = jnp.maximum(inter_log, jnp.max(D, -1))
    P = jnp.exp(D - m[..., None]) * jnp.einsum('bhncd,bhnsd->bhncs', qc, kc)
    w_inter = jnp.exp(inter_log - m)
    num = jnp.einsum('bhncs,bhnse->bhnce', P, vc) + w_inter[..., None] * jnp.einsum('bhncd,bhnde->bhnce', qc, C_prev)
    den = jnp.sum(P, -1) + w_inter * jnp.einsum('bhncd,bhnd->bhnc', qc, n_prev)
    h = num / jnp.maximum(jnp.abs(den), jnp.exp(-m))[..., None]
    return h.reshape(B, H, S, d)

def even_mixer(x, w_in, w_out, rel_bias):
    h = x @ w_in
    q_r, k_r, v_r, g_r, q_d, k_d, v_d = jnp.split(h, list(EVEN_SPLITS), axis=-1)
    y_r = retention(split_heads(q_r, RET_HEADS), split_heads(k_r, RET_HEADS), split_heads(v_r, RET_HEADS))
    y_r = merge_heads(head_norm(y_r)) * jax.nn.silu(g_r.astype(jnp.float32))
    y_d = merge_heads(dilated_attention(split_heads(q_d, DSA_HEADS), split_heads(k_d, DSA_HEADS), split_heads(v_d, DSA_HEADS), rel_bias))
    y = jnp.concatenate([y_r, y_d], axis=-1).astype(x.dtype)
    return y @ w_out

def odd_mixer(x, w_in, gate_b, conv_w, w_out):
    h = x @ w_in
    qk, v, o, gates = jnp.split(h, list(ODD_SPLITS), axis=-1)
    qk = jax.nn.silu(causal_dwconv(qk, conv_w))
    q, k = jnp.split(qk, 2, axis=-1)
    gates = gates.astype(jnp.float32) + gate_b
    log_i = gates[..., :MLSTM_HEADS].transpose(0, 2, 1)
    log_f = jax.nn.log_sigmoid(gates[..., MLSTM_HEADS:]).transpose(0, 2, 1)
    y = mlstm(split_heads(q, MLSTM_HEADS), split_heads(k, MLSTM_HEADS), split_heads(v, MLSTM_HEADS), log_i, log_f)
    y = merge_heads(y) * jax.nn.sigmoid(o.astype(jnp.float32))
    return y.astype(x.dtype) @ w_out

def conv_ffn(x, w_up, conv_w, conv_b, w_down):
    gate, up = jnp.split(x @ w_up, 2, axis=-1)
    act = jax.nn.silu(causal_dwconv(gate, conv_w) + conv_b)
    return (act * up) @ w_down

def second_inputs(seed: int = 0) -> dict:
    key = jax.random.key(seed)
    ks = jax.random.split(key, 16)
    f32 = jnp.float32

    def nrm(k, shape, scale):
        return jax.random.normal(k, shape, f32) * scale

    d_in = D_MODEL ** -0.5
    x = nrm(ks[0], (BATCH, SEQ, D_MODEL), 1.0)
    even_scale = np.ones(EVEN_IN, np.float32)
    even_scale[2 * RET_W:3 * RET_W] = DEEPNORM_BETA
    even_scale[4 * RET_W + 2 * DSA_W:] = DEEPNORM_BETA
    even_w_in = nrm(ks[1], (N_EVEN_2, D_MODEL, EVEN_IN), d_in) * jnp.asarray(even_scale)
    even_w_out = nrm(ks[2], (N_EVEN_2, MIX_W_EVEN, D_MODEL), MIX_W_EVEN ** -0.5 * DEEPNORM_BETA)
    rel_bias = nrm(ks[3], (T5_BUCKETS, DSA_HEADS), 0.5)
    odd_scale = np.ones(ODD_IN, np.float32)
    odd_scale[2 * MLSTM_W:3 * MLSTM_W] = DEEPNORM_BETA
    odd_w_in = nrm(ks[4], (N_ODD_2, D_MODEL, ODD_IN), d_in) * jnp.asarray(odd_scale)
    i_bias = nrm(ks[5], (N_ODD_2, MLSTM_HEADS), 0.1)
    f_bias = jnp.linspace(3.0, 6.0, MLSTM_HEADS, dtype=f32) + nrm(ks[6], (N_ODD_2, MLSTM_HEADS), 0.1)
    odd_gate_b = jnp.concatenate([i_bias, f_bias], axis=-1)
    odd_conv_w = nrm(ks[7], (N_ODD_2, MLSTM_CONV, 2 * MLSTM_W), MLSTM_CONV ** -0.5)
    odd_w_out = nrm(ks[8], (N_ODD_2, MLSTM_W, D_MODEL), MLSTM_W ** -0.5 * DEEPNORM_BETA)
    ffn_w_up = nrm(ks[9], (DEPTH, D_MODEL, 2 * D_FF), d_in * DEEPNORM_BETA)
    ffn_conv_w = nrm(ks[10], (DEPTH, FFN_CONV, D_FF), FFN_CONV ** -0.5)
    ffn_conv_b = nrm(ks[11], (DEPTH, D_FF), 0.02)
    ffn_w_down = nrm(ks[12], (DEPTH, D_FF, D_MODEL), D_FF ** -0.5 * DEEPNORM_BETA)
    ln_g = 1.0 + nrm(ks[13], (DEPTH, 2, D_MODEL), 0.02)
    ln_b = nrm(ks[14], (DEPTH, 2, D_MODEL), 0.02)
    return {"x": x, "even_w_in": even_w_in, "even_w_out": even_w_out, "rel_bias": rel_bias, "odd_w_in": odd_w_in, "odd_gate_b": odd_gate_b, "odd_conv_w": odd_conv_w, "odd_w_out": odd_w_out, "ffn_w_up": ffn_w_up, "ffn_conv_w": ffn_conv_w, "ffn_conv_b": ffn_conv_b, "ffn_w_down": ffn_w_down, "ln_g": ln_g, "ln_b": ln_b}

def second_block(x, even_w_in, even_w_out, rel_bias, odd_w_in, odd_gate_b, odd_conv_w, odd_w_out, ffn_w_up, ffn_conv_w, ffn_conv_b, ffn_w_down, ln_g, ln_b):
    for layer in range(DEPTH):
        j = layer // 2
        if layer % 2 == 0:
            mix = even_mixer(x, even_w_in[j], even_w_out[j], rel_bias)
        else:
            mix = odd_mixer(x, odd_w_in[j], odd_gate_b[j], odd_conv_w[j], odd_w_out[j])
        x = layer_norm(DEEPNORM_ALPHA * x + mix, ln_g[layer, 0], ln_b[layer, 0])
        ffn = conv_ffn(x, ffn_w_up[layer], ffn_conv_w[layer], ffn_conv_b[layer], ffn_w_down[layer])
        x = layer_norm(DEEPNORM_ALPHA * x + ffn, ln_g[layer, 1], ln_b[layer, 1])
    return x


def setup_inputs(seed=0):
    out = dict(first_inputs(seed))
    for name, value in second_inputs(seed + 1).items():
        if name != "x":
            out[name + "_2"] = value
    return out


def reference(
    x, c, ctx, c_ctx, w_ada, b_ada, norm_mix, norm_ffn, norm_final, ab_w_in, ab_w_out,
    mla_q_norm, mla_w_q_up, mla_kv_norm, mla_w_kv_up, gqa_q_norm, gqa_k_norm, na_w_in, na_w_out,
    na_rpb, moe_w_rg, moe_b_rg, moe_w_re, moe_b_re, moe_w_gate, moe_w_up, moe_w_down,
    even_w_in_2, even_w_out_2, rel_bias_2, odd_w_in_2, odd_gate_b_2, odd_conv_w_2, odd_w_out_2,
    ffn_w_up_2, ffn_conv_w_2, ffn_conv_b_2, ffn_w_down_2, ln_g_2, ln_b_2,
):
    x = first_block(
        x, c, ctx, c_ctx, w_ada, b_ada, norm_mix, norm_ffn, norm_final, ab_w_in, ab_w_out,
        mla_q_norm, mla_w_q_up, mla_kv_norm, mla_w_kv_up, gqa_q_norm, gqa_k_norm, na_w_in,
        na_w_out, na_rpb, moe_w_rg, moe_b_rg, moe_w_re, moe_b_re, moe_w_gate, moe_w_up,
        moe_w_down,
    )
    return second_block(
        x, even_w_in_2, even_w_out_2, rel_bias_2, odd_w_in_2, odd_gate_b_2, odd_conv_w_2,
        odd_w_out_2, ffn_w_up_2, ffn_conv_w_2, ffn_conv_b_2, ffn_w_down_2, ln_g_2, ln_b_2,
    )


_drawn_inputs = setup_inputs


def setup_inputs(seed=0):
    import zlib

    import numpy as np

    out = dict(_drawn_inputs(seed))
    spreads = {}
    factors = {'norm_mix': 2.919,
     'mla_q_norm': 5.634,
     'mla_kv_norm': 3.095,
     'gqa_q_norm': 6.619,
     'gqa_k_norm': 6.248,
     'na_rpb': 8.0,
     'moe_b_rg': 8.0,
     'moe_b_re': 4.073,
     'rel_bias_2': 6.45,
     'odd_conv_w_2': 5.348,
     'ffn_conv_b_2': 8.0}
    for name, (base, spread) in spreads.items():
        noise = np.random.default_rng([zlib.crc32(name.encode()), seed]).standard_normal(out[name].shape)
        drawn = base * np.exp(spread * noise) if base else spread * noise
        out[name] = __import__('jax').numpy.asarray(drawn.astype(out[name].dtype))
    for name, factor in factors.items():
        out[name] = (out[name] * factor).astype(out[name].dtype)
    return out
```

```python
import math
from contextlib import ExitStack

import numpy as np
import concourse.bass as bass
from concourse import mybir

F32 = mybir.dt.float32
F32R = mybir.dt.float32r
I32 = mybir.dt.int32
ACT = mybir.ActivationFunctionType
ALU = mybir.AluOpType
AX = mybir.AxisListType

PART = 128
BANK = 512
D = 1024
DC = D // PART
CTX, SEQ = 256, 512
TOK = CTX + SEQ
CTX_T, SEQ_T, TOK_T = CTX // PART, SEQ // PART, TOK // PART
LAT = slice(CTX, TOK)
DEPTH = 2
GRID_W = 64
ROWS = SEQ // GRID_W
H_A, NOPE_A, ROPE_A, V_A, Q_LORA, KV_LORA = 8, 64, 32, 64, 384, 256
QK_A = NOPE_A + ROPE_A
H_B, KV_B, HEAD = 8, 2, 64
AB_IN = Q_LORA + KV_LORA + ROPE_A + H_B * HEAD + 2 * KV_B * HEAD
H_C, WIN_R, WIN_C = 16, 8, 16
REL_R, REL_C = 2 * WIN_R - 1, 2 * WIN_C - 1
BAND_ROWS = PART
N_GROUPS, PER_GROUP, N_EXPERTS, D_EXPERT = 4, 8, 32, 512
EC = D_EXPERT // PART
SLOTS = 128
RET_H, RET_D = 4, 128
DSA_H = 8
T5_BUCKETS, T5_MAX = 32, 2048
DSA_PATTERNS = ((128, 1), (512, 4), (2048, 16))
ML_H, ML_D, ML_CONV = 4, 256, 4
D_FF, FFN_CONV = 2816, 3
FC = D_FF // PART
ALPHA = (2.0 * DEPTH) ** 0.25
RMS_EPS, LN_EPS = 1e-6, 1e-5
MASKED = -1e30

PARAM_BLOCKS = (
    (("c", 8), ("c_ctx", 8), ("b_ada", 96), ("norm_mix", 16)),
    (("norm_ffn", 16), ("norm_final", 8), ("mla_q_norm", 3), ("mla_kv_norm", 2), ("gqa_q_norm", 1),
     ("gqa_k_norm", 1), ("ln_g_2", 32), ("ln_b_2", 32)),
    (("odd_conv_w_2", 64), ("ffn_conv_b_2", 44)),
    (("ffn_conv_w_2:0", 66),),
    (("ffn_conv_w_2:1", 66),),
)


def param_columns():
    at = {}
    for b, entries in enumerate(PARAM_BLOCKS):
        r = 0
        for name, rows in entries:
            at[name] = b * PART + r
            r += rows
    return at


def rope_rows(rot_dim):
    n = rot_dim // 4
    inv = (np.float32(10000.0) ** (-np.arange(n, dtype=np.float32) / np.float32(n))).astype(np.float32)
    t = np.arange(SEQ)
    r, c = (t // GRID_W).astype(np.float32), (t % GRID_W).astype(np.float32)
    ang = np.concatenate([r[:, None] * inv, c[:, None] * inv], -1)
    return np.repeat(ang.T, 2, axis=0).astype(np.float32)


def pair_swap(n):
    m = np.zeros((n, n), np.float32)
    for i in range(0, n, 2):
        m[i + 1, i] = -1.0
        m[i, i + 1] = 1.0
    return m


def t5_bucket(dist):
    exact = T5_BUCKETS // 2
    n = np.maximum(dist, 0)
    large = exact + (np.log(np.maximum(n, 1).astype(np.float32) / np.float32(exact)) / np.float32(math.log(T5_MAX / exact))
                     * np.float32(T5_BUCKETS - exact)).astype(np.int32)
    return np.where(n < exact, n, np.minimum(large, T5_BUCKETS - 1))


def shape_constants():
    k = {}
    k["ident"] = np.eye(PART, dtype=np.float32)
    k["ones"] = np.ones((PART, PART), np.float32)
    k["half_ones"] = np.kron(np.eye(2, dtype=np.float32), np.ones((64, 64), np.float32))
    swap_a = np.zeros((PART, QK_A), np.float32)
    swap_a[NOPE_A:QK_A, NOPE_A:] = pair_swap(ROPE_A)
    ang_a = np.concatenate([np.zeros((NOPE_A, SEQ), np.float32), rope_rows(ROPE_A)], 0)
    ang_b = np.tile(rope_rows(HEAD), (2, 1))
    pad = np.zeros((PART - QK_A, SEQ), np.float32)
    k["swap_a"], k["swap_b"] = swap_a, pair_swap(PART)
    k["rope_a"] = np.stack([np.concatenate([np.cos(ang_a), pad]), np.concatenate([np.sin(ang_a), pad])], 1)
    k["rope_b"] = np.stack([np.cos(ang_b), np.sin(ang_b)], 1)
    k["earlier"] = np.triu(np.ones((PART, PART), np.float32), 1)
    k["count"] = np.tile(np.arange(PART, dtype=np.float32), (PART, 1))
    k["token"] = (np.arange(TOK_T, dtype=np.float32)[None, :] * PART + np.arange(PART, dtype=np.float32)[:, None])
    at, band = np.arange(3 * GRID_W - 1)[None, :], np.zeros((BAND_ROWS, 3 * GRID_W - 1), np.float32)
    for odd in range(2):
        band[odd * GRID_W:odd * GRID_W + REL_C] = np.arange(REL_C)[:, None] + at == GRID_W * (1 + odd) - 1 + REL_C // 2
    k["band"] = band
    col = np.arange(GRID_W)
    start = np.clip(col - WIN_C // 2, 0, GRID_W - WIN_C)[:, None]
    inside = (col[None, :] >= start) & (col[None, :] < start + WIN_C)
    k["outside"] = np.tile(np.where(inside, 0.0, MASKED).astype(np.float32), (2, 1))
    half = RET_D // 2
    inv = (np.float32(1.0) / (np.float32(10000.0) ** (np.arange(0, RET_D, 2, dtype=np.float32) / np.float32(RET_D)))).astype(np.float32)
    ang = np.tile((np.arange(SEQ, dtype=np.float32)[:, None] * inv[None, :]).T, (2, 1)).astype(np.float32)
    k["rope_r"] = np.stack([np.cos(ang), np.sin(ang)], 1)
    k["swap_r"] = np.zeros((RET_D, RET_D), np.float32)
    for i in range(half):
        k["swap_r"][i + half, i] = -1.0
        k["swap_r"][i, i + half] = 1.0
    log_gamma = np.log1p(-np.exp2(-5.0 - np.arange(RET_H)))
    rel = np.arange(SEQ)[None, :] - np.arange(PART)[:, None]
    k["decay"] = np.where(rel >= 0, np.exp(log_gamma[:, None, None] * np.maximum(rel, 0)), 0.0).transpose(1, 0, 2).astype(np.float32)
    dist = SEQ - 1 - np.arange(SEQ + PART)
    k["by_bucket"] = ((t5_bucket(dist)[None, :] == np.arange(PART)[:, None]) & (dist >= 0)).astype(np.float32)
    apart = SEQ - PART + np.arange(PART)[:, None] - np.arange(SEQ)[None, :]
    seen = sum(((apart >= 0) & (apart <= w) & (apart % r == 0)).astype(np.float64) for w, r in DSA_PATTERNS)
    k["seen"] = np.where(seen > 0, np.log(np.maximum(seen, 1.0)), MASKED).astype(np.float32)
    k["future"] = np.where(np.arange(PART)[None, :] >= np.arange(PART)[:, None], 0.0, MASKED).astype(np.float32)
    k["row"] = np.repeat(np.eye(ML_H, dtype=np.float32)[:, :, None], PART, 2)
    return {name: np.ascontiguousarray(a, np.float32) for name, a in k.items()}


class NormJob:

    def __init__(self, n, src, dst, gain, bias, sums, size, gated=None):
        self.gated = gated
        self.n, self.src, self.dst, self.gain, self.bias, self.sums, self.inv_n = n, src, dst, gain, bias, sums, 1.0 / size


class Load:

    def __init__(self, slot, source, ring, after):
        self.slot, self.source, self.ring, self.after = slot, source, ring, after


class Ready:

    def __init__(self, ahead):
        self.ahead, self.ring, self.after = ahead, None, None


class Product:

    def __init__(self, operands, shape, take, load, engine, finish):
        self.operands, self.shape, self.take, self.load, self.engine, self.finish = operands, shape, take, load, engine, finish


class Ahead:

    def __init__(self, P, pieces):
        P.ahead_loads += len(pieces)
        self.pieces, self.arrived, self.into = pieces, 16 * P.ahead_loads, P.ahead_in

    def start(self, sp):
        for slot, source in self.pieces:
            sp.dma_start(slot, source).then_inc(self.into, 16)

    def wait(self, eng):
        eng.wait_ge(self.into, self.arrived)


class QueryGroup:

    def __init__(self, tiles, first):
        self.tiles, self.first = tiles, first


class Link:

    def __init__(self, eng, sem):
        self.eng, self.sem, self.n = eng, sem, 0

    def __call__(self, ins):
        self.n += 1
        ins.then_inc(self.sem, 1)
        self.eng.wait_ge(self.sem, self.n)


def scope(nc, ctx, tag):
    sems = []

    def release():
        for s in sems:
            nc.gpsimd.sem_clear(s)
            nc.release_semaphore(s)

    ctx.callback(release)

    def sb(name, shape, dt=F32):
        return ctx.enter_context(nc.sbuf_tensor(f"{tag}_{name}", shape, dt))

    def ps(name, shape):
        return ctx.enter_context(nc.psum_tensor(f"{tag}_{name}", shape, F32))

    def sem(name):
        sems.append(nc.alloc_semaphore(f"{tag}_{name}"))
        return sems[-1]

    return sb, ps, sem


def load_stage(nc, A, K, P):
    with ExitStack() as ctx:
        sb, ps, sem = scope(nc, ctx, "load")
        tokens = sb("tokens", [PART, TOK_T, D])
        rows = sb("rows", [PART, len(PARAM_BLOCKS), PART])
        turned = [ps(f"turned{n}", [PART, 4, PART]) for n in range(4)]
        const_in, tokens_in, rows_in = sem("const_in"), sem("tokens_in"), sem("rows_in")
        turned_ready, act_done, dve_done = sem("turned_ready"), sem("act_done"), sem("dve_done")
        silu_done, eps_set = sem("silu_done"), sem("eps_set")
        block = ctx.enter_context(nc.Block())
        n_const = 0
        n_rows = 0

        @block.sync
        def _(sp):
            nonlocal n_const
            for name, tile in (("ident", P.ident), ("ones", P.ones), ("half_ones", P.half_ones)):
                sp.dma_start(tile[:], K[name]).then_inc(const_in, 16)
                n_const += 16
            sp.dma_start(tokens[:, 0:CTX_T, :], A["ctx"][0].rearrange("(t p) d -> p t d", p=PART)).then_inc(tokens_in, 16)
            sp.dma_start(tokens[:, CTX_T:, :], A["x"][0].rearrange("(t p) d -> p t d", p=PART)).then_inc(tokens_in, 16)

        vectors = {
            "c": A["c"].rearrange("a (r p) -> (a r) p", p=PART),
            "c_ctx": A["c_ctx"].rearrange("(r p) -> r p", p=PART),
            "odd_conv_w_2": A["odd_conv_w_2"].rearrange("a k (r p) -> (a k r) p", p=PART),
            "ln_g_2": A["ln_g_2"].rearrange("a b (r p) -> (a b r) p", p=PART),
            "ln_b_2": A["ln_b_2"].rearrange("a b (r p) -> (a b r) p", p=PART),
            "norm_final": A["norm_final"].rearrange("(r p) -> r p", p=PART),
            "ffn_conv_w_2:0": A["ffn_conv_w_2"][0].rearrange("k (r p) -> (k r) p", p=PART),
            "ffn_conv_w_2:1": A["ffn_conv_w_2"][1].rearrange("k (r p) -> (k r) p", p=PART),
        }
        for name in ("b_ada", "norm_mix", "norm_ffn", "mla_q_norm", "mla_kv_norm", "ffn_conv_b_2"):
            vectors[name] = A[name].rearrange("a (r p) -> (a r) p", p=PART)
        used = [sum(n for _, n in entries) for entries in PARAM_BLOCKS]
        n_turns = TOK_T * 2 + len(PARAM_BLOCKS)

        def take(n):
            if n < TOK_T * 2:
                t, half = n // 2, n % 2
                return P.x[:, half * 4:half * 4 + 4, t * PART:(t + 1) * PART], turned[n % 4][:]
            b = n - TOK_T * 2
            return P.cols[:, b * PART:b * PART + used[b]], turned[n % 4][:, 0, 0:used[b]]

        last_param = n_turns - len(PARAM_BLOCKS)

        @block.scalar
        def _(act):
            nonlocal n_rows
            for b, entries in enumerate(PARAM_BLOCKS):
                r = 0
                for name, n in entries:
                    if name.startswith("gqa"):
                        for half in (0, HEAD):
                            act.dma_start(rows[r:r + 1, b, half:half + HEAD], A[name]).then_inc(rows_in, 16)
                            n_rows += 16
                    else:
                        act.dma_start(rows[r:r + n, b, :], vectors[name]).then_inc(rows_in, 16)
                        n_rows += 16
                    r += n
            for n in range(0, n_turns, 2):
                act.wait_ge(turned_ready, n + 1)
                out, got = take(n)
                nc.scalar.activation(out, got, ACT.Copy).then_inc(act_done, 1)
            act.wait_ge((act_done, dve_done)[last_param % 2], last_param // 2 + 1)
            for w, name in enumerate(("c", "c_ctx")):
                at = P.col[name]
                nc.scalar.activation(P.cond[:, :, w], P.cols[:, at:at + DC], ACT.Silu).then_inc(silu_done, 1)

        @block.tensor
        def _(pe):
            pe.wait_ge(const_in, n_const)
            pe.wait_ge(tokens_in, 32)
            for n in range(n_turns):
                if n >= 4:
                    pe.wait_ge((act_done, dve_done)[n % 2], (n - 4) // 2 + 1)
                if n < TOK_T * 2:
                    t, half = n // 2, n % 2
                    for c in range(4):
                        at = (half * 4 + c) * PART
                        last = nc.tensor.transpose(turned[n % 4][:, c, :], tokens[:, t, at:at + PART], P.ident[:])
                else:
                    b = n - TOK_T * 2
                    if b == 0:
                        pe.wait_ge(rows_in, n_rows)
                    last = nc.tensor.transpose(turned[n % 4][:, 0, 0:used[b]], rows[0:used[b], b, :],
                                               P.ident[0:used[b], 0:used[b]])
                last.then_inc(turned_ready, 1)

        @block.vector
        def _(dve):
            nc.vector.memset(P.eps[:, 0:1], RMS_EPS).then_inc(eps_set, 1)
            nc.vector.memset(P.eps[:, 1:2], LN_EPS).then_inc(eps_set, 1)
            nc.vector.memset(P.zero[:], 0.0).then_inc(eps_set, 1)
            for n in range(1, n_turns, 2):
                dve.wait_ge(turned_ready, n + 1)
                out, got = take(n)
                nc.vector.tensor_copy(out, got).then_inc(dve_done, 1)


def conditioning_stage(nc, A, P):
    SLABS = 6 * D // BANK
    SLOTS_IN = 4
    TURNS = SLABS // SLOTS_IN
    with ExitStack() as ctx:
        sb, ps, sem = scope(nc, ctx, "ada")
        slab = [sb(f"slab{s}", [PART, DC, BANK]) for s in range(SLOTS_IN)]
        rows = sb("rows", [2, DEPTH, 6 * D])
        acc = [ps(f"acc{s}", [2, BANK]) for s in range(SLOTS_IN)]
        turned = [ps(f"turned{l}", [PART, BANK])[:, 0:12 * DC].rearrange("p (c w) -> p c w", w=2) for l in range(DEPTH)]
        slab_in = [sem(f"slab_in{s}") for s in range(SLOTS_IN)]
        acc_ready, acc_taken, turned_ready, biased, scaled = (
            sem(n) for n in ("acc_ready", "acc_taken", "turned_ready", "biased", "scaled"))
        block = ctx.enter_context(nc.Block())

        @block.sync
        def _(sp):
            for l in range(DEPTH):
                w = rows_of(A["w_ada"][l])
                if l == 0:
                    for s in range(SLOTS_IN):
                        sp.dma_start(slab[s][:], w[:, :, s * BANK:(s + 1) * BANK]).then_inc(slab_in[s], 16)
                with sp.Fori(1 if l == 0 else 0, TURNS) as i:
                    for s in range(SLOTS_IN):
                        sp.wait_ge(acc_ready, (i + l * TURNS) * SLOTS_IN + s + 1 - SLOTS_IN)
                        sp.dma_start(slab[s][:], w[:, :, bass.ds((i * SLOTS_IN + s) * BANK, BANK)]).then_inc(slab_in[s], 16)

        @block.tensor
        def _(pe):
            for l in range(DEPTH):
                with pe.Fori(0, TURNS) as i:
                    for s in range(SLOTS_IN):
                        pe.wait_ge(slab_in[s], (i + l * TURNS) * 16 + 16)
                        pe.wait_ge(acc_taken, (i + l * TURNS) * SLOTS_IN + s + 1)
                        for c in range(DC):
                            last = nc.tensor.matmul(acc[s][:], P.cond[:, c, :], slab[s][:, c, :], start=c == 0, stop=c == DC - 1)
                        last.then_inc(acc_ready, 1)
                pe.wait_ge(acc_taken, (l + 1) * SLABS + SLOTS_IN)
                for c in range(6 * DC):
                    last = nc.tensor.transpose(turned[l][:, c, :], rows[:, l, c * PART:(c + 1) * PART], P.ident[0:2, 0:2])
                last.then_inc(turned_ready, 1)

        @block.scalar
        def _(act):
            act.sem_inc(acc_taken, SLOTS_IN)
            for l in range(DEPTH):
                with act.Fori(0, TURNS) as i:
                    for s in range(SLOTS_IN):
                        act.wait_ge(acc_ready, (i + l * TURNS) * SLOTS_IN + s + 1)
                        nc.scalar.activation(rows[:, l, bass.ds((i * SLOTS_IN + s) * BANK, BANK)], acc[s][:], ACT.Copy).then_inc(acc_taken, 1)

        @block.vector
        def _(dve):
            for l in range(DEPTH):
                at = P.col["b_ada"] + l * 6 * DC
                dve.wait_ge(turned_ready, l + 1)
                nc.vector.tensor_tensor(P.mod[:, l], turned[l], P.cols[:, at:at + 6 * DC].unsqueeze(2).to_broadcast([PART, 6 * DC, 2]),
                                        ALU.add).then_inc(biased, 1)
            dve.wait_ge(biased, DEPTH)
            for l in range(DEPTH):
                for n, (name, sc) in enumerate((("norm_mix", 1), ("norm_ffn", 4))):
                    at = P.col[name] + l * DC
                    gain = P.cols[:, at:at + DC].unsqueeze(2).to_broadcast([PART, DC, 2])
                    nc.vector.scalar_tensor_tensor(P.scale[:, l, n, :, :], P.mod[:, l, sc * DC:(sc + 1) * DC, :], 1.0, gain,
                                                   ALU.add, ALU.mult).then_inc(scaled, 1)
            at = P.col["gqa_q_norm"]
            nc.vector.tensor_scalar(P.gq_gain[:], P.cols[:, at:at + 1], HEAD ** -0.5, None, ALU.mult).then_inc(scaled, 1)


def norm_stage(nc, P, tag, jobs, eps, center=False, ahead=None):
    C = max(len(j.src) for j in jobs)
    with ExitStack() as ctx:
        sb, ps, sem = scope(nc, ctx, tag)
        n_sq = 2 if C < DC else 1
        squares = [sb(f"squares{n}", [PART, C, BANK]) for n in range(n_sq)]
        root = [sb(f"root{n}", [PART, BANK]) for n in range(2)]
        total = [ps(f"total{n}", [PART, BANK]) for n in range(2)]
        mean = [ps(f"mean{n}", [PART, BANK]) for n in range(2)]
        squared, summed, rooted, inverted = sem("squared"), sem("summed"), sem("rooted"), sem("inverted")
        scaled, mean_ready, centered, shifted = sem("scaled"), sem("mean_ready"), sem("centered"), sem("shifted")
        gated = sem("gated")
        block = ctx.enter_context(nc.Block())
        first = np.cumsum([0] + [len(j.src) for j in jobs]).tolist()

        if ahead is not None:
            @block.sync
            def _(sp):
                ahead.start(sp)

        @block.scalar
        def _(act):
            for n, j in enumerate(jobs):
                if n >= n_sq:
                    act.wait_ge(summed, n - n_sq + 1)
                for c, src in enumerate(j.src):
                    if center:
                        act.wait_ge(centered, first[n] + c + 1)
                    nc.scalar.activation(squares[n % n_sq][:, c, 0:j.n], j.dst[c] if center else src, ACT.Square).then_inc(squared, 1)
                act.wait_ge(summed, n + 1)
                if n >= 2:
                    act.wait_ge(scaled, first[n - 1])
                nc.scalar.activation(root[n % 2][:, 0:j.n], total[n % 2][:, 0:j.n], ACT.Sqrt, scale=j.inv_n,
                                     bias=P.eps[:, eps:eps + 1]).then_inc(rooted, 1)
                if j.bias is not None:
                    for c, dst in enumerate(j.dst):
                        act.wait_ge(scaled, first[n] + c + 1)
                        nc.scalar.activation(dst, dst, ACT.Identity, bias=j.bias[c]).then_inc(shifted, 1)

        @block.tensor
        def _(pe):
            for n, j in enumerate(jobs):
                if center:
                    if n >= 2:
                        pe.wait_ge(centered, first[n - 1])
                    for c, src in enumerate(j.src):
                        last = nc.tensor.matmul(mean[n % 2][:, 0:j.n], j.sums[:], src, start=c == 0, stop=c == len(j.src) - 1)
                    last.then_inc(mean_ready, 1)
                if n >= 2:
                    pe.wait_ge(rooted, n - 1)
                for c in range(len(j.src)):
                    pe.wait_ge(squared, first[n] + c + 1)
                    last = nc.tensor.matmul(total[n % 2][:, 0:j.n], j.sums[:], squares[n % n_sq][:, c, 0:j.n],
                                            start=c == 0, stop=c == len(j.src) - 1)
                last.then_inc(summed, 1)

        @block.vector
        def _(dve):
            for n, j in enumerate(jobs):
                if center:
                    dve.wait_ge(mean_ready, n + 1)
                    for c, src in enumerate(j.src):
                        nc.vector.scalar_tensor_tensor(j.dst[c], mean[n % 2][:, 0:j.n], -j.inv_n, src, ALU.mult, ALU.add).then_inc(centered, 1)
                dve.wait_ge(rooted, n + 1)
                nc.vector.reciprocal(root[n % 2][:, 0:j.n], root[n % 2][:, 0:j.n]).then_inc(inverted, 1)
                dve.wait_ge(inverted, n + 1)
                if center:
                    dve.wait_ge(squared, first[n + 1])
                for c, src in enumerate(j.src):
                    nc.vector.scalar_tensor_tensor(j.dst[c], j.dst[c] if center else src, j.gain[c], root[n % 2][:, 0:j.n],
                                                   ALU.mult, ALU.mult).then_inc(scaled, 1)
                if j.gated is not None:
                    dve.wait_ge(scaled, first[n + 1])
                    for c, (gate, dst) in enumerate(zip(*j.gated)):
                        nc.vector.tensor_tensor(dst, j.dst[c], gate, ALU.mult).then_inc(gated, 1)


def modulate_jobs(P, l, which, spans):
    return [NormJob(
        n=t.stop - t.start,
        src=[P.x[:, c, t] for c in range(DC)],
        dst=[P.h[:, c, t] for c in range(DC)],
        gain=[P.scale[:, l, which, c, w:w + 1] for c in range(DC)],
        bias=[P.mod[:, l, 3 * which * DC + c, w:w + 1] for c in range(DC)],
        sums=P.ones, size=D,
    ) for t, w in spans]


def split_products(operands):
    return [pair for l_hi, l_lo, r_hi, r_lo in operands for pair in ((l_hi, r_hi), (l_hi, r_lo), (l_lo, r_hi))]


HALF_SLAB = BANK // 2


def raw_slab(P, n):
    return P.ahead[:].rearrange("p (s a) (b n) -> p s (a b) n", s=2, n=HALF_SLAB)[:, n % 2]


class SplitProduct:

    def __init__(self, slab, operands, shape, take, engine=None, finish=None):
        self.slab, self.operands, self.shape, self.take, self.engine, self.finish = slab, operands, shape, take, engine, finish


def split_stage(nc, P, tag, x, slabs, products, first, engines=("act", "dve"), banks=8):
    n_x = x.shape[-1]
    with ExitStack() as ctx:
        sb, ps, sem = scope(nc, ctx, tag)
        x_hi, x_lo = (sb(f"x_{part}", [PART, DC, n_x], F32R) for part in ("hi", "lo"))
        w_hi, w_lo = ([sb(f"w_{part}{n}", [PART, DC, HALF_SLAB], F32R) for n in range(2)] for part in ("hi", "lo"))
        bank = [ps(f"bank{b}", [PART, BANK]) for b in range(banks)]
        raw_in = [sem(f"raw_in{n}") for n in range(2)]
        x_rounded, x_split, w_rounded, w_split = sem("x_rounded"), sem("x_split"), sem("w_rounded"), sem("w_split")
        ready, step, finished = sem("ready"), sem("step"), sem("finished")
        taken = {e: sem(f"taken_{e}") for e in engines}
        block = ctx.enter_context(nc.Block())
        engine_of = [p.engine or engines[n % len(engines)] for n, p in enumerate(products)]
        turn = [engine_of[:n].count(e) for n, e in enumerate(engine_of)]
        starts = [min(n for n, p in enumerate(products) if p.slab == h) for h in range(len(slabs))] + [len(products)]
        arrivals = [16 * sum(len(slabs[m]) for m in range(h % 2, h + 1, 2) if m >= 2) for h in range(len(slabs))]

        @block.sync
        def _(sp):
            for h in range(2, len(slabs)):
                sp.wait_ge(w_split, h - 1)
                for slot, source in slabs[h]:
                    sp.dma_start(slot, source).then_inc(raw_in[h % 2], 16)

        def result(n):
            rows, cols = products[n].shape
            return bank[n % banks][0:rows, 0:cols]

        @block.tensor
        def _(pe):
            for n, p in enumerate(products):
                if n == starts[p.slab]:
                    pe.wait_ge(w_split, p.slab + 1)
                if n >= banks:
                    m = n - banks
                    pe.wait_ge(taken[engine_of[m]], turn[m] + 1)
                w, x_parts = (w_hi[p.slab % 2], w_lo[p.slab % 2]), (x_hi, x_lo)
                parts = [p.operands(w[i], x_parts[j]) for i, j in ((0, 0), (0, 1), (1, 0))]
                for c in range(DC):
                    if n == 0:
                        pe.wait_ge(x_split, c + 1)
                    for k, part in enumerate(parts):
                        last = nc.tensor.matmul(result(n), *part[c], start=c == 0 and k == 0, stop=c == DC - 1 and k == len(parts) - 1)
                last.then_inc(ready, 1)

        @block.vector
        def _(dve):
            V = nc.vector
            link = Link(dve, step)

            def split(h):
                if h < 2:
                    first.wait(dve)
                else:
                    dve.wait_ge(raw_in[h % 2], arrivals[h])
                    dve.wait_ge(ready, starts[h - 1])
                V.tensor_copy(w_hi[h % 2][:], raw_slab(P, h)).then_inc(w_rounded, 1)
                dve.wait_ge(w_rounded, h + 1)
                V.tensor_tensor(w_lo[h % 2][:], raw_slab(P, h), w_hi[h % 2][:].bitcast(F32), ALU.subtract).then_inc(w_split, 1)

            split(0)
            for c in range(DC):
                V.tensor_copy(x_hi[:, c, :], x[:, c, :]).then_inc(x_rounded, 1)
            for c in range(DC):
                dve.wait_ge(x_rounded, c + 1)
                V.tensor_tensor(x_lo[:, c, :], x[:, c, :], x_hi[:, c, :].bitcast(F32), ALU.subtract).then_inc(x_split, 1)
            for n, p in enumerate(products):
                if n == starts[p.slab] and p.slab + 1 < len(slabs):
                    split(p.slab + 1)
                if engine_of[n] == "dve":
                    dve.wait_ge(ready, n + 1)
                    p.take("dve", result(n), link).then_inc(taken["dve"], 1)

        if "act" in engines:
            @block.scalar
            def _(act):
                for n, p in enumerate(products):
                    if engine_of[n] == "act":
                        act.wait_ge(ready, n + 1)
                        p.take("act", result(n), None).then_inc(taken["act"], 1)
                    if p.finish is not None:
                        act.wait_ge(taken["dve"], turn[n] + 1)
                        p.finish().then_inc(finished, 1)


def half_slabs(P, w):
    return [[(raw_slab(P, n), rows_of(w)[:, :, n * HALF_SLAB:(n + 1) * HALF_SLAB])] for n in range(w.shape[-1] // HALF_SLAB)]


def feature_slab(nc, products, slab, dst, spans, scale=None, func=None):
    for j in range(HALF_SLAB // PART):
        for t in spans:
            out = dst(j)[:, t]
            products.append(SplitProduct(
                slab, lambda w, x, j=j, t=t: [(w[:, c, j * PART:(j + 1) * PART], x[:, c, t]) for c in range(DC)],
                (PART, t.stop - t.start), activated(nc, out, func) if func else copy_to(nc, out, scale), "act" if func else None))


def token_slab(nc, products, slab, dst, tiles):
    for t in range(tiles):
        products.append(SplitProduct(
            slab, lambda w, x, t=t: [(x[:, c, t * PART:(t + 1) * PART], w[:, c, :]) for c in range(DC)],
            (PART, HALF_SLAB), copy_to(nc, dst(t))))


def product_stage(nc, P, tag, loads, products, engines=("act", "dve"), banks=8, ahead=None):
    with ExitStack() as ctx:
        sb, ps, sem = scope(nc, ctx, tag)
        bank = [ps(f"bank{b}", [PART, BANK]) for b in range(banks)]
        rings = sorted({ld.ring for ld in loads if ld.ring is not None})
        loaded = {r: sem(f"loaded{r}") for r in rings}
        ready = sem("ready")
        taken = {e: sem(f"taken_{e}") for e in engines}
        step, finished = sem("step"), sem("finished")
        block = ctx.enter_context(nc.Block())
        engine_of = [p.engine or engines[n % len(engines)] for n, p in enumerate(products)]
        turn = [engine_of[:n].count(e) for n, e in enumerate(engine_of)]
        arrivals = []
        for n, ld in enumerate(loads):
            arrivals.append(16 * sum(m.ring == ld.ring for m in loads[:n + 1]))

        @block.sync
        def _(sp):
            if ahead is not None:
                ahead.start(sp)
            for ld in loads:
                if ld.ring is None:
                    continue
                if ld.after is not None:
                    sp.wait_ge(ready, ld.after + 1)
                sp.dma_start(ld.slot, ld.source).then_inc(loaded[ld.ring], 16)

        def result(n):
            p = products[n]
            p0, rows, cols = p.shape
            return bank[n % banks][p0:p0 + rows, 0:cols]

        @block.tensor
        def _(pe):
            have = -1
            for n, p in enumerate(products):
                if have < p.load:
                    for ld in loads[have + 1:p.load + 1]:
                        if ld.ring is None:
                            ld.ahead.wait(pe)
                    for r in rings:
                        last = [m for m in range(have + 1, p.load + 1) if loads[m].ring == r][-1:]
                        if last:
                            pe.wait_ge(loaded[r], arrivals[last[0]])
                    have = p.load
                if n >= banks:
                    m = n - banks
                    pe.wait_ge(taken[engine_of[m]], turn[m] + 1)
                for k, (lhs_t, rhs) in enumerate(p.operands):
                    last = nc.tensor.matmul(result(n), lhs_t, rhs, start=k == 0, stop=k == len(p.operands) - 1)
                last.then_inc(ready, 1)

        if "act" in engines:
            @block.scalar
            def _(act):
                for n, p in enumerate(products):
                    if engine_of[n] == "act":
                        act.wait_ge(ready, n + 1)
                        p.take("act", result(n), None).then_inc(taken["act"], 1)
                    if p.finish is not None:
                        act.wait_ge(taken["dve"], turn[n] + 1)
                        p.finish().then_inc(finished, 1)

        if "dve" in engines:
            @block.vector
            def _(dve):
                link = Link(dve, step)
                for n, p in enumerate(products):
                    if engine_of[n] == "dve":
                        dve.wait_ge(ready, n + 1)
                        p.take("dve", result(n), link).then_inc(taken["dve"], 1)


def copy_to(nc, dst, scale=None):
    def take(engine, result, link):
        if engine == "act":
            return nc.scalar.activation(dst, result, ACT.Copy, scale=1.0 if scale is None else scale)
        if scale is None:
            return nc.vector.tensor_copy(dst, result)
        return nc.vector.tensor_scalar(dst, result, scale, None, ALU.mult)
    return take


def activated(nc, dst, func):
    def take(engine, result, link):
        return nc.scalar.activation(dst, result, func)
    return take


def add_scaled(nc, x, gate):
    def take(engine, result, link):
        return nc.vector.scalar_tensor_tensor(x, result, gate, x, ALU.mult, ALU.add)
    return take


def add_deep(nc, x):
    def take(engine, result, link):
        return nc.vector.scalar_tensor_tensor(x, x, ALPHA, result, ALU.mult, ALU.add)
    return take


def load(slot, source, ring=0, after=None):
    return Load(slot, source, ring, after)


def product(operands, shape, take, load=0, engine=None, finish=None):
    return Product(operands, shape, take, load, engine, finish)


def wide(t):
    return [slice(0, CTX), slice(CTX, TOK)] if t == TOK else [LAT]


def rows_of(w):
    return w.rearrange("(c p) n -> p c n", p=PART)


def rope_stage(nc, P, tag, K, items, spread=None, also=None):
    with ExitStack() as ctx:
        sb, ps, sem = scope(nc, ctx, tag)
        kinds = sorted({kind for _, _, _, kind in items})
        swap = {"swap_" + n: sb("swap_" + n, list(K["swap_" + n].shape)) for n in kinds}
        table = {"rope_" + n: sb("rope_" + n, [PART, 2, SEQ]) for n in kinds}
        turned = [ps(f"turned{n}", [PART, BANK]) for n in range(2)]
        by_cos = [sb(f"by_cos{n}", [PART, BANK]) for n in range(2)]
        by_sin = [sb(f"by_sin{n}", [PART, BANK]) for n in range(2)]
        tables_in, swapped, parts, rotated, copied = sem("tables_in"), sem("swapped"), sem("parts"), sem("rotated"), sem("copied")
        block = ctx.enter_context(nc.Block())

        @block.sync
        def _(sp):
            for n in swap:
                sp.dma_start(swap[n][:], K[n]).then_inc(tables_in, 16)
            for n in table:
                sp.dma_start(table[n][:], K[n]).then_inc(tables_in, 16)
            if also is not None:
                also(sp)

        @block.tensor
        def _(pe):
            pe.wait_ge(tables_in, 32 * len(kinds))
            for n, (x, p0, rows, kind) in enumerate(items):
                if n >= 2:
                    pe.wait_ge(rotated, n - 1)
                nc.tensor.matmul(turned[n % 2][p0:p0 + rows, :], swap["swap_" + kind][p0:p0 + rows, p0:p0 + rows], x,
                                 start=True, stop=True).then_inc(swapped, 1)

        @block.vector
        def _(dve):
            dve.wait_ge(tables_in, 32 * len(kinds))
            for n, (x, p0, rows, kind) in enumerate(items):
                r = slice(p0, p0 + rows)
                cos, sin = table["rope_" + kind][r, 0, :], table["rope_" + kind][r, 1, :]
                nc.vector.tensor_tensor(by_cos[n % 2][r, :], x, cos, ALU.mult).then_inc(parts, 1)
                dve.wait_ge(swapped, n + 1)
                nc.vector.tensor_tensor(by_sin[n % 2][r, :], turned[n % 2][r, :], sin, ALU.mult).then_inc(parts, 1)
                dve.wait_ge(parts, 2 * n + 2)
                nc.vector.tensor_tensor(x, by_cos[n % 2][r, :], by_sin[n % 2][r, :], ALU.add).then_inc(rotated, 1)

        if spread:
            @block.scalar
            def _(act):
                act.wait_ge(rotated, len(items))
                for src, dst in spread:
                    nc.scalar.activation(dst, src, ACT.Copy).then_inc(copied, 1)


class HeadPairs:

    def __init__(self, rows, halves, pairs, sources, keys, out, bias=None):
        self.rows, self.halves, self.pairs, self.sources, self.keys, self.out, self.bias = rows, halves, pairs, sources, keys, out, bias
        self.before = 0
        self.q = None

    def own(self, s):
        return slice(s * HEAD, (s + 1) * HEAD) if self.halves else slice(0, self.rows)


def each_turn(eng, runs, body):
    for r, run in enumerate(runs):
        if run.pairs > 1:
            with eng.Fori(0, run.pairs - 1) as i:
                body(run, i, run, i + 1)
        body(run, run.pairs - 1, runs[r + 1] if r + 1 < len(runs) else None, 0)


def attention_stage(nc, P, tag, runs, groups, n_keys, ahead=None):
    steps = [(g, t) for g, grp in enumerate(groups) for t in range(len(grp.tiles))]
    NT, G = len(steps), len(groups)
    U, V = 2 * NT, 2 * G
    n_q = sum(len(g.tiles) for g in groups) * PART
    KC = n_keys // PART
    biased = runs[0].bias is not None
    for r in range(1, len(runs)):
        runs[r].before = runs[r - 1].before + runs[r - 1].pairs
    if biased:
        per_tile = [len(runs[0].bias(0, u // NT, steps[u % NT][1])) for u in range(U)]
        bias_steps = [sum(per_tile[:u + 1]) for u in range(U)]
    with ExitStack() as ctx:
        sb, ps, sem = scope(nc, ctx, tag)
        for r, run in enumerate(runs):
            run.q = [sb(f"q{r}{s}", [run.rows, n_q]) for s in range(2)]
        cleared = sem("cleared")
        v = [sb(f"v{s}", [PART, KC, HEAD]) for s in range(2)]
        probs = [sb(f"probs{n}", [PART, n_keys]) for n in range(2)]
        raised = [sb(f"raised{n}", [PART, n_keys]) for n in range(2)]
        probs_t = [[sb(f"probs_t{s}{g}", [PART, KC if len(grp.tiles) > 2 else CTX_T, len(grp.tiles) * PART])
                    for g, grp in enumerate(groups)] for s in range(2)]
        top = sb("top", [PART, 2])
        mass = sb("mass", [PART, 2])
        share = sb("share", [PART, 2])
        scores = [ps(f"scores{n}", [PART, 2 * BANK]) for n in range(2)]
        turned = ps("turned", [PART, 2 * BANK])
        mixed = [ps(f"mixed{n}", [PART, BANK]) for n in range(2)]
        staged = [sem(f"staged{s}") for s in range(2)]
        scores_ready, scores_free, biased_ready = sem("scores_ready"), sem("scores_free"), sem("biased_ready")
        top_ready, exp_ready, share_ready = sem("top_ready"), sem("exp_ready"), sem("share_ready")
        probs_ready, turned_ready, turned_taken = sem("probs_ready"), sem("turned_ready"), sem("turned_taken")
        mixed_ready, mixed_taken = sem("mixed_ready"), sem("mixed_taken")
        block = ctx.enter_context(nc.Block())

        def two_on(run, i, after, j, u):
            if u + 2 < U:
                return run, i, u + 2
            return None if after is None else (after, j, u + 2 - U)

        @block.sync
        def _(sp):
            def stage_head(run, i, s):
                queries, values = run.sources(i, s)
                sp.dma_start(run.q[s][run.own(s), :], queries).then_inc(staged[s], 16)
                sp.dma_start(v[s][:], values).then_inc(staged[s], 16)

            def stage_pair(run, i):
                for s in range(2):
                    sp.wait_ge(mixed_taken, (i + run.before) * V + (s + 1) * G - V + 2)
                    stage_head(run, i, s)

            for r, run in enumerate(runs):
                if r == 0:
                    for s in range(2):
                        stage_head(run, 0, s)
                    if ahead is not None:
                        ahead.start(sp)
                else:
                    stage_pair(run, 0)
                if run.pairs > 1:
                    with sp.Fori(1, run.pairs) as i:
                        stage_pair(run, i)

        @block.tensor
        def _(pe):
            pe.sem_inc(turned_ready, 2)

            def score(run, i, u):
                s, n = u // NT, u % NT
                g, t = steps[n]
                query, keys = groups[g].tiles[t]
                n_turn = i + run.before
                if n == 0:
                    pe.wait_ge(staged[s], n_turn * 32 + 32)
                pe.wait_ge(scores_free, n_turn * U + u + 1)
                for at in range(0, keys, BANK):
                    w = min(BANK, keys - at)
                    last = nc.tensor.matmul(scores[u % 2][:, at:at + w], run.q[s][:, query:query + PART], run.keys(i, s)[..., at:at + w],
                                            start=True, stop=True)
                last.then_inc(scores_ready, 1)

            def body(run, i, after, j):
                n_turn = i + run.before

                def turn(u):
                    g, t = steps[u % NT]
                    keys = groups[g].tiles[t][1]
                    pe.wait_ge(probs_ready, n_turn * U + u + 3)
                    pe.wait_ge(turned_taken, n_turn * U + u + 1)
                    for c in range(keys // PART):
                        last = nc.tensor.transpose(turned[:, c * PART:(c + 1) * PART], probs[u % 2][:, c * PART:(c + 1) * PART],
                                                   P.ident[:])
                    last.then_inc(turned_ready, 1)

                def mix(m, u):
                    s, g = m // G, m % G
                    grp = groups[g]
                    last_keys = max(keys for _, keys in grp.tiles) // PART
                    pe.wait_ge(turned_taken, n_turn * U + u + 2)
                    pe.wait_ge(mixed_taken, n_turn * V + m + 1)
                    for c in range(last_keys):
                        f = grp.first(c) * PART
                        end = len(grp.tiles) * PART
                        last = nc.tensor.matmul(mixed[m % 2][s * HEAD:(s + 1) * HEAD, f:end], v[s][:, c, :],
                                                probs_t[s][g][:, c, f:end], start=c == 0, stop=c == last_keys - 1)
                    last.then_inc(mixed_ready, 1)

                waiting = None
                m = 0
                for u in range(U):
                    coming = two_on(run, i, after, j, u)
                    if coming:
                        score(*coming)
                    turn(u)
                    if waiting is not None:
                        mix(m, waiting)
                        m, waiting = m + 1, None
                    g, t = steps[u % NT]
                    if t == len(groups[g].tiles) - 1:
                        waiting = u
                mix(m, waiting)

            pe.wait_ge(cleared, 2 * len(runs))
            score(runs[0], 0, 0)
            score(runs[0], 0, 1)
            each_turn(pe, runs, body)

        @block.scalar
        def _(act):
            act.sem_inc(turned_taken, 1)
            act.sem_inc(mixed_taken, 2)
            if not biased:
                act.sem_inc(scores_free, 2)

            def exponent(run, i, u):
                g, t = steps[u % NT]
                keys = groups[g].tiles[t][1]
                n_tile = (i + run.before) * U + u
                act.wait_ge(top_ready, n_tile + 1)
                if not biased:
                    act.wait_ge(probs_ready, n_tile + 1)
                src = raised[u % 2] if biased else scores[u % 2]
                ins = nc.scalar.activation(raised[u % 2][:, 0:keys], src[:, 0:keys], ACT.Exp, bias=top[:, u % 2:u % 2 + 1],
                                           accum_out=mass[:, u % 2:u % 2 + 1])
                ins.then_inc(exp_ready, 1)
                if not biased:
                    act.wait_ge(exp_ready, n_tile + 1)
                    act.sem_inc(scores_free, 1)

            def body(run, i, after, j):
                n_turn = i + run.before

                def copy_turned(u):
                    s, n = u // NT, u % NT
                    g, t = steps[n]
                    keys = groups[g].tiles[t][1]
                    act.wait_ge(turned_ready, n_turn * U + u + 3)
                    nc.scalar.activation(probs_t[s][g][:, 0:keys // PART, t * PART:(t + 1) * PART],
                                         turned[:, 0:keys].rearrange("p (c q) -> p c q", q=PART), ACT.Copy).then_inc(turned_taken, 1)

                def take(m):
                    s, g = m // G, m % G
                    act.wait_ge(mixed_ready, n_turn * V + m + 1)
                    n = len(groups[g].tiles) * PART
                    nc.scalar.activation(run.out(i, s, groups[g].tiles[0][0], n), mixed[m % 2][s * HEAD:(s + 1) * HEAD, 0:n],
                                         ACT.Copy).then_inc(mixed_taken, 1)

                waiting = False
                m = 0
                for u in range(U):
                    coming = two_on(run, i, after, j, u)
                    if coming:
                        exponent(*coming)
                    copy_turned(u)
                    if waiting:
                        take(m)
                        m, waiting = m + 1, False
                    g, t = steps[u % NT]
                    waiting = t == len(groups[g].tiles) - 1
                take(m)

            exponent(runs[0], 0, 0)
            exponent(runs[0], 0, 1)
            each_turn(act, runs, body)

        @block.vector
        def _(dve):
            if biased:
                dve.sem_inc(scores_free, 2)
            dve.sem_inc(probs_ready, 2)

            def find_top(run, i, u):
                s, n = u // NT, u % NT
                g, t = steps[n]
                keys = groups[g].tiles[t][1]
                n_turn = i + run.before
                dve.wait_ge(scores_ready, n_turn * U + u + 1)
                src = scores[u % 2]
                if biased:
                    dve.wait_ge(probs_ready, n_turn * U + u + 1)
                    src = raised[u % 2]
                    for at, w, table in run.bias(i, s, t):
                        dst, raw = src[:, at:at + w], scores[u % 2][:, at:at + w]
                        if table is None:
                            nc.vector.tensor_copy(dst, raw).then_inc(biased_ready, 1)
                        elif len(table.shape) == 3:
                            r = table.shape[1]
                            nc.vector.tensor_tensor(dst.rearrange("p (r c) -> p r c", r=r), raw.rearrange("p (r c) -> p r c", r=r),
                                                    table, ALU.add).then_inc(biased_ready, 1)
                        else:
                            nc.vector.tensor_tensor(dst, raw, table, ALU.add).then_inc(biased_ready, 1)
                    dve.wait_ge(biased_ready, n_turn * bias_steps[U - 1] + bias_steps[u])
                    dve.sem_inc(scores_free, 1)
                nc.vector.tensor_reduce(top[:, u % 2:u % 2 + 1], src[:, 0:keys], AX.X, ALU.max, negate=True).then_inc(top_ready, 1)

            def body(run, i, after, j):
                n_turn = i + run.before

                def normalise(u):
                    g, t = steps[u % NT]
                    keys = groups[g].tiles[t][1]
                    dve.wait_ge(exp_ready, n_turn * U + u + 1)
                    nc.vector.reciprocal(share[:, u % 2:u % 2 + 1], mass[:, u % 2:u % 2 + 1]).then_inc(share_ready, 1)
                    dve.wait_ge(share_ready, n_turn * U + u + 1)
                    dve.wait_ge(turned_ready, n_turn * U + u + 1)
                    nc.vector.tensor_scalar(probs[u % 2][:, 0:keys], raised[u % 2][:, 0:keys], share[:, u % 2:u % 2 + 1], None,
                                            ALU.mult).then_inc(probs_ready, 1)

                for u in range(U):
                    normalise(u)
                    coming = two_on(run, i, after, j, u)
                    if coming:
                        find_top(*coming)

            for run in runs:
                for s in range(2):
                    if run.halves:
                        nc.vector.memset(run.q[s][run.own(1 - s), :], 0.0).then_inc(cleared, 1)
                    else:
                        dve.sem_inc(cleared, 1)
            find_top(runs[0], 0, 0)
            find_top(runs[0], 0, 1)
            each_turn(dve, runs, body)


def latent_mixer(nc, A, K, P, first, ahead):
    with ExitStack() as ctx:
        sb, _, _ = scope(nc, ctx, "l0")
        qa = sb("qa", [QK_A, H_A, TOK])
        ka = sb("ka", [QK_A, H_A, TOK])
        va = sb("va", [PART, TOK_T, H_A * V_A])
        gq = sb("gq", [PART, H_B // 2, TOK])
        gk = sb("gk", [PART, TOK])
        gv = sb("gv", [PART, TOK_T, KV_B * HEAD])
        spans = wide(TOK)
        with ExitStack() as low:
            sb, _, _ = scope(nc, low, "low")
            QC, KVC = Q_LORA // PART, KV_LORA // PART
            cq, ckv = sb("cq", [PART, QC, TOK]), sb("ckv", [PART, KVC, TOK])
            kr = sb("kr", [QK_A, TOK])
            with ExitStack() as wide_in:
                sb, _, _ = scope(nc, wide_in, "ab_in")
                GROUPS = ((BANK, Q_LORA + KV_LORA + ROPE_A), (AB_IN - 2 * KV_B * HEAD, AB_IN))
                rest = sb("w", [PART, DC, AB_IN - BANK])
                w = rows_of(A["ab_w_in"][0])
                loads = [Ready(first)] + [load(rest[:, :, a - BANK:b - BANK], w[:, :, a:b], ring=n) for n, (a, b) in enumerate(GROUPS)]
                heads, at_q = H_B // KV_B, Q_LORA + KV_LORA + ROPE_A
                q_slot = rest[:, :, at_q - BANK:at_q - BANK + H_B * HEAD].rearrange("p c (h k e) -> p c h k e", k=KV_B, e=HEAD)
                q_rows = w[:, :, at_q:at_q + H_B * HEAD].rearrange("p c (k h e) -> p c h k e", k=KV_B, e=HEAD)
                for h in range(heads):
                    for n in range(KV_B):
                        loads.append(load(q_slot[:, :, h, n], q_rows[:, :, h, n], ring=2))
                products = []

                def feature_rows(columns, p0, dst, t, n_load):
                    rows = columns(0).shape[-1]
                    products.append(product([(columns(c), P.h[:, c, t]) for c in range(DC)],
                                            (p0, rows, t.stop - t.start), copy_to(nc, dst), n_load))

                def span(at, rows):
                    return lambda c: P.ahead[:, c, at:at + rows] if at < BANK else rest[:, c, at - BANK:at - BANK + rows]

                for t in spans:
                    for j in range(QC):
                        feature_rows(span(j * PART, PART), 0, cq[:, j, t], t, 0)
                    for j in range(KVC):
                        feature_rows(span(Q_LORA + j * PART, PART), 0, ckv[:, j, t], t, int(Q_LORA + j * PART >= BANK))
                last = len(loads) - 1
                for t in spans:
                    feature_rows(span(Q_LORA + KV_LORA, ROPE_A), NOPE_A, kr[NOPE_A:QK_A, t], t, 1)
                    feature_rows(span(at_q + H_B * HEAD, PART), 0, gk[:, t], t, 2)
                    for j in range(heads):
                        feature_rows(span(at_q + j * PART, PART), 0, gq[:, j, t], t, last)
                at = AB_IN - KV_B * HEAD
                for t in range(TOK_T):
                    products.append(product([(P.h[:, c, t * PART:(t + 1) * PART], rest[:, c, at - BANK:]) for c in range(DC)],
                                            (0, PART, KV_B * HEAD), copy_to(nc, gv[:, t, :]), 2))
                product_stage(nc, P, "ab_in", loads, products)

            def norm_jobs(x, chunks, gain, sums, size):
                return [NormJob(n=t.stop - t.start, src=[x[:, c, t] for c in cs], dst=[x[:, c, t] for c in cs],
                                gain=[gain(c) for c in cs], bias=None, sums=sums, size=size) for t in spans for cs in chunks]

            def col(name):
                return lambda c: P.cols[:, P.col[name] + c:P.col[name] + c + 1]

            norm_stage(nc, P, "norm_qk",
                       norm_jobs(cq, [range(QC)], col("mla_q_norm"), P.ones, Q_LORA)
                       + norm_jobs(ckv, [range(KVC)], col("mla_kv_norm"), P.ones, KV_LORA)
                       + norm_jobs(gq, [[c] for c in range(H_B // 2)], lambda c: P.gq_gain[:], P.half_ones, HEAD)
                       + norm_jobs(gk[:].unsqueeze(1), [[0]], col("gqa_k_norm"), P.half_ones, HEAD), 0)

            with ExitStack() as up:
                sb, _, _ = scope(nc, up, "ab_up")
                wq = sb("wq", [PART, QC, H_A * QK_A])
                wkv = sb("wkv", [PART, KVC, H_A * (NOPE_A + V_A)])
                loads = [load(wq[:], rows_of(A["mla_w_q_up"][0]), 0), load(wkv[:], rows_of(A["mla_w_kv_up"][0]), 1)]
                products = []
                for h in range(H_A):
                    for t in spans:
                        n = t.stop - t.start
                        products.append(product([(wq[:, c, h * QK_A:(h + 1) * QK_A], cq[:, c, t]) for c in range(QC)],
                                                (0, QK_A, n), copy_to(nc, qa[:, h, t], QK_A ** -0.5), 0))
                for h in range(H_A):
                    at = h * (NOPE_A + V_A)
                    for t in spans:
                        n = t.stop - t.start
                        products.append(product([(wkv[:, c, at:at + NOPE_A], ckv[:, c, t]) for c in range(KVC)],
                                                (0, NOPE_A, n), copy_to(nc, ka[0:NOPE_A, h, t]), 1))
                wv = wkv[:].rearrange("p c (h e) -> p c h e", h=H_A)
                for t in range(TOK_T):
                    products.append(product([(ckv[:, c, t * PART:(t + 1) * PART], wv[:, c, :, NOPE_A:]) for c in range(KVC)],
                                            (0, PART, H_A * V_A), copy_to(nc, va[:, t, :]), 1))
                product_stage(nc, P, "ab_up", loads, products)

            items = [(kr[NOPE_A:QK_A, LAT], NOPE_A, ROPE_A, "a")]
            items += [(qa[:, h, LAT], 0, QK_A, "a") for h in range(H_A)]
            items += [(gq[:, c, LAT], 0, PART, "b") for c in range(H_B // 2)]
            items += [(gk[:, LAT], 0, PART, "b")]
            spread = [(kr[NOPE_A:QK_A, :], ka[NOPE_A:QK_A, h, :]) for h in range(H_A)]
            rope_stage(nc, P, "rope", K, items, spread, lambda sp: clear_rows(P, sp))

        def group(q0, tiles, keys):
            return QueryGroup(tiles=[(q0 + t * PART, keys) for t in range(tiles)], first=lambda c: 0)

        groups = [group(0, CTX_T, CTX), group(CTX, SEQ_T, TOK)]
        P.o = P.h

        def source_a(i, s):
            h = i * 2 + s
            return qa[:, bass.ds(h, 1), :], va[:, :, bass.ds(h * V_A, V_A)]

        def out_a(i, s, q0, n):
            return P.o[s * HEAD:(s + 1) * HEAD, bass.ds(i, 1), q0:q0 + n]

        def source_b(i, s):
            return gq[s * HEAD:(s + 1) * HEAD, bass.ds(i, 1), :], gv[:, :, s * HEAD:(s + 1) * HEAD]

        def out_b(i, s, q0, n):
            return P.o[s * HEAD:(s + 1) * HEAD, bass.ds(i + H_A // 2, 1), q0:q0 + n]

        attention_stage(nc, P, "attn", [
            HeadPairs(QK_A, False, H_A // 2, source_a, lambda i, s: ka[:, bass.ds(i * 2 + s, 1), :], out_a),
            HeadPairs(PART, True, H_B // 2, source_b, lambda i, s: gk[:], out_b),
        ], groups, TOK, ahead)


def ab_out_slabs(P, w):
    rows_a, rows_b = H_A * V_A, w[H_A * V_A:].rearrange("(k h e) n -> k e h n", k=KV_B, e=HEAD)

    def pieces(n):
        slot, cols = raw_slab(P, n), slice(n * HALF_SLAB, (n + 1) * HALF_SLAB)
        return [(slot[:, 0:rows_a // PART, :], rows_of(w[0:rows_a, cols]))] + [
            (slot[k * HEAD:(k + 1) * HEAD, rows_a // PART:, :], rows_b[k, :, :, cols]) for k in range(KV_B)]
    return [pieces(n) for n in range(D // HALF_SLAB)]


def out_stage(nc, P, tag, slabs, o, spans, take, first):
    products = []
    for j in range(DC):
        slab, at = divmod(j * PART, HALF_SLAB)
        for t in spans:
            products.append(SplitProduct(slab, lambda w, x, at=at, t=t: [(w[:, c, at:at + PART], x[:, c, t]) for c in range(DC)],
                                         (PART, t.stop - t.start), take(j, t)))
    split_stage(nc, P, tag, o, slabs, products, first, engines=("dve",))


def extra_blocks(n_tok):
    return (2 * n_tok - 2) // SLOTS


BLOCKS_MAX = N_EXPERTS + extra_blocks(TOK)


def expert_stage(nc, A, K, P, l, first_tok):
    n_tok = TOK - first_tok
    NT = n_tok // PART
    EXTRA = extra_blocks(n_tok)
    BLOCKS = N_EXPERTS + EXTRA
    LOGITS = N_GROUPS + N_EXPERTS
    tag = f"moe{l}"
    with ExitStack() as ctx:
        sb, _, sem = scope(nc, ctx, tag)
        w_gate = [sb(f"w_gate{s}", [PART, DC, D_EXPERT]) for s in range(2)]
        w_up = [sb(f"w_up{s}", [PART, DC, D_EXPERT]) for s in range(2)]
        w_down = [sb(f"w_down{s}", [PART, EC, D]) for s in range(2)]
        slot_token = sb("slot_token", [SLOTS, BLOCKS], I32)
        row_of = sb("row_of", [PART, NT, 2], I32)
        weight = sb("weight", [PART, NT, 2])
        extra_expert = sb("extra_expert", [PART, EXTRA], I32)
        n_extra = sb("n_extra", [PART, 1], I32)
        wide_in = [sem(f"wide_in{s}") for s in range(2)]
        down_in = [sem(f"down_in{s}") for s in range(2)]

        def expert_weights(sp, s, e):
            sp.dma_start(w_gate[s][:], A["moe_w_gate"][l, e].rearrange("a (p c) n -> p (a c) n", c=DC)).then_inc(wide_in[s], 16)
            sp.dma_start(w_up[s][:], A["moe_w_up"][l, e].rearrange("a (p c) n -> p (a c) n", c=DC)).then_inc(wide_in[s], 16)

        def route():
            with ExitStack() as ctx:
                sb, ps, sem = scope(nc, ctx, tag + "r")
                w_route = sb("w_route", [PART, DC, LOGITS])
                b_route = sb("b_route", [PART, LOGITS])
                earlier, count, token = sb("earlier", [PART, PART]), sb("count", [PART, PART]), sb("token", [PART, TOK_T])
                ROWS = 4
                h_rows = P.ahead[:].rearrange("p (n a) b -> p n (a b)", n=ROWS)
                turned = [ps(f"turned{n}", [PART, D]) for n in range(2)]
                logits_ps = ps("logits_ps", [PART, BANK])[:, 0:NT * LOGITS].rearrange("p (t n) -> p t n", t=NT)
                rank_ps, count_ps = (ps(n, [PART, BANK])[:, 0:NT * N_EXPERTS].rearrange("p (t n) -> p t n", n=N_EXPERTS)
                                     for n in ("rank_ps", "count_ps"))
                slot_ps = ps("slot_ps", [PART, BANK])[0:SLOTS, 0:BLOCKS]
                ranks = sb("ranks", [PART, NT, N_EXPERTS])
                before = sb("before", [PART, NT + 1, N_EXPERTS])
                logits = sb("logits", [PART, NT, LOGITS])
                chosen = sb("chosen", [PART, 2, NT, N_EXPERTS])
                either = sb("either", [PART, NT, N_EXPERTS])
                open_e = sb("open_e", [PART, NT, N_EXPERTS])
                work = sb("work", [PART, NT, N_EXPERTS])
                top = sb("top", [PART, 3, NT])
                index = sb("index", [PART, 3, NT])
                group_hot = sb("group_hot", [PART, NT, N_GROUPS])
                group_exp = sb("group_exp", [PART, NT, N_GROUPS])
                group_mass, gap, share = sb("group_mass", [PART, NT]), sb("gap", [PART, NT]), sb("share", [PART, 3, NT])
                rank, turn, place, block_of, more = (sb(n, [PART, 2, NT]) for n in ("rank", "turn", "place", "block_of", "more"))
                blocks_after, blocks_before = (sb(n, [PART, N_EXPERTS]) for n in ("blocks_after", "blocks_before"))
                extra_of = sb("extra_of", [PART, N_EXPERTS])
                ended = sb("ended", [PART, EXTRA, N_EXPERTS])
                extra_f = sb("extra_f", [PART, EXTRA])
                slot_hot = sb("slot_hot", [PART, 2, NT, SLOTS])
                token_in_block = sb("token_in_block", [PART, 2, NT, BLOCKS])
                consts_in, turned_ready, rows_act, rows_dve = sem("consts_in"), sem("turned_ready"), sem("rows_act"), sem("rows_dve")
                rows_out = [sem(f"rows_out{n}") for n in range(ROWS)]
                placed = sem("placed")
                logits_ready, chosen_ready, rank_ready, hot_ready, slots_ready, slots_taken = (
                    sem(n) for n in ("logits_ready", "chosen_ready", "rank_ready", "hot_ready", "slots_ready", "slots_taken"))
                step, group_ready, group_expd, gap_ready, gap_expd = (
                    sem(n) for n in ("step", "group_ready", "group_expd", "gap_ready", "gap_expd"))
                block = ctx.enter_context(nc.Block())

                @block.sync
                def _(sp):
                    sp.dma_start(w_route[:, :, 0:N_GROUPS], rows_of(A["moe_w_rg"][l])).then_inc(consts_in, 16)
                    sp.dma_start(w_route[:, :, N_GROUPS:], rows_of(A["moe_w_re"][l])).then_inc(consts_in, 16)
                    sp.dma_start(b_route[:, 0:N_GROUPS], A["moe_b_rg"][l:l + 1, :].to_broadcast([PART, N_GROUPS])).then_inc(consts_in, 16)
                    sp.dma_start(b_route[:, N_GROUPS:], A["moe_b_re"][l:l + 1, :].to_broadcast([PART, N_EXPERTS])).then_inc(consts_in, 16)
                    for name, t in (("earlier", earlier), ("count", count), ("token", token)):
                        sp.dma_start(t[:], K[name]).then_inc(consts_in, 16)
                    for t in range(NT):
                        sp.wait_ge(rows_act, t + 1)
                        sp.wait_ge(rows_dve, t + 1)
                        sp.dma_start(P.h_dram[t * PART:(t + 1) * PART, :], h_rows[:, t % ROWS]).then_inc(rows_out[t % ROWS], 16)
                    for s in range(2):
                        expert_weights(sp, s, bass.ds(s, 1))
                        sp.dma_start(w_down[s][:], rows_of(A["moe_w_down"][l, s])).then_inc(down_in[s], 16)
                    sp.wait_ge(P.rows_cleared, CLEARED)
                    for n in range(ROWS):
                        sp.wait_ge(rows_out[n], 16 * len(range(n, NT, ROWS)))

                @block.tensor
                def _(pe):
                    for t in range(NT):
                        at = first_tok + t * PART
                        if t >= 2:
                            pe.wait_ge(rows_act, t - 1)
                            pe.wait_ge(rows_dve, t - 1)
                        for c in range(DC):
                            last = nc.tensor.transpose(turned[t % 2][:, c * PART:(c + 1) * PART], P.h[:, c, at:at + PART], P.ident[:])
                        last.then_inc(turned_ready, 1)
                    pe.wait_ge(consts_in, 7 * 16)
                    for t in range(NT):
                        at = first_tok + t * PART
                        for c in range(DC):
                            last = nc.tensor.matmul(logits_ps[:, t, :], P.h[:, c, at:at + PART], w_route[:, c, :],
                                                    start=c == 0, stop=c == DC - 1)
                    last.then_inc(logits_ready, 1)
                    pe.wait_ge(chosen_ready, 1)
                    nc.tensor.matmul(rank_ps, earlier[:], either[:], start=True, stop=True)
                    last = nc.tensor.matmul(count_ps, P.ones[:], either[:], start=True, stop=True)
                    last.then_inc(rank_ready, 1)
                    pe.wait_ge(hot_ready, 4 * NT)
                    for n in range(2 * NT):
                        j, t = divmod(n, NT)
                        last = nc.tensor.matmul(slot_ps, slot_hot[:, j, t, :], token_in_block[:, j, t, :],
                                                start=n == 0, stop=n == 2 * NT - 1)
                    last.then_inc(slots_ready, 1)

                @block.gpsimd
                def _(pool):
                    pool.wait_ge(consts_in, 7 * 16)
                    for j in range(2):
                        pool.wait_ge(placed, j + 1)
                        for t in range(NT):
                            nc.gpsimd.tensor_scalar(token_in_block[:, j, t, :], count[:, 0:BLOCKS], block_of[:, j, t:t + 1], token[:, t:t + 1],
                                                    ALU.is_equal, ALU.mult).then_inc(hot_ready, 1)

                @block.scalar
                def _(act):
                    for t in range(NT):
                        act.wait_ge(turned_ready, t + 1)
                        if t >= ROWS:
                            act.wait_ge(rows_out[t % ROWS], 16 * (t // ROWS))
                        nc.scalar.activation(h_rows[:, t % ROWS, 0:BANK], turned[t % 2][:, 0:BANK], ACT.Copy).then_inc(rows_act, 1)
                    act.wait_ge(group_ready, 1)
                    nc.scalar.activation(group_exp[:], group_exp[:], ACT.Exp).then_inc(group_expd, 1)
                    act.wait_ge(gap_ready, 1)
                    nc.scalar.activation(gap[:], gap[:], ACT.Exp).then_inc(gap_expd, 1)

                @block.vector
                def _(dve):
                    for t in range(NT):
                        dve.wait_ge(turned_ready, t + 1)
                        if t >= ROWS:
                            dve.wait_ge(rows_out[t % ROWS], 16 * (t // ROWS))
                        nc.vector.tensor_copy(h_rows[:, t % ROWS, BANK:D], turned[t % 2][:, BANK:D]).then_inc(rows_dve, 1)
                    link = Link(dve, step)
                    V = nc.vector

                    def over(a, n):
                        return a.unsqueeze(2).to_broadcast([PART, NT, n])

                    def first_largest(values, n, m, hot):
                        numbers = count[:, 0:n].unsqueeze(1).to_broadcast([PART, NT, n])
                        tmp = work[:, :, 0:n]
                        link(V.tensor_reduce(top[:, m, :], values, AX.X, ALU.max))
                        link(V.tensor_tensor(tmp, values, over(top[:, m, :], n), ALU.not_equal))
                        link(V.scalar_tensor_tensor(tmp, tmp, float(PART), numbers, ALU.mult, ALU.add))
                        link(V.tensor_reduce(index[:, m, :], tmp, AX.X, ALU.min))
                        link(V.tensor_tensor(hot, numbers, over(index[:, m, :], n), ALU.is_equal))

                    dve.wait_ge(consts_in, 7 * 16)
                    dve.wait_ge(logits_ready, 1)
                    link(V.tensor_tensor(logits[:], logits_ps, b_route[:].unsqueeze(1).to_broadcast([PART, NT, LOGITS]), ALU.add))
                    groups, experts = logits[:, :, 0:N_GROUPS], logits[:, :, N_GROUPS:]
                    first_largest(groups, N_GROUPS, 2, group_hot[:])
                    V.tensor_tensor(group_exp[:], groups, over(top[:, 2, :], N_GROUPS), ALU.subtract).then_inc(group_ready, 1)
                    link(V.tensor_scalar(group_hot[:], group_hot[:], -1.0, -MASKED, ALU.add, ALU.mult))
                    link(V.tensor_tensor(open_e[:].rearrange("p t (g e) -> p t g e", g=N_GROUPS),
                                         experts.rearrange("p t (g e) -> p t g e", g=N_GROUPS),
                                         group_hot[:].unsqueeze(3).to_broadcast([PART, NT, N_GROUPS, PER_GROUP]), ALU.add))
                    first_largest(open_e[:], N_EXPERTS, 0, chosen[:, 0])
                    link(V.scalar_tensor_tensor(open_e[:], chosen[:, 0], 4 * MASKED, open_e[:], ALU.mult, ALU.add))
                    first_largest(open_e[:], N_EXPERTS, 1, chosen[:, 1])
                    V.tensor_tensor(either[:], chosen[:, 0], chosen[:, 1], ALU.add).then_inc(chosen_ready, 1)
                    V.tensor_tensor(gap[:], top[:, 1, :], top[:, 0, :], ALU.subtract).then_inc(gap_ready, 1)
                    dve.wait_ge(group_expd, 1)
                    link(V.tensor_reduce(group_mass[:], group_exp[:], AX.X, ALU.add))
                    dve.wait_ge(gap_expd, 1)
                    link(V.tensor_scalar(share[:, 0, :], gap[:], 1.0, None, ALU.add))
                    link(V.tensor_tensor(share[:, 1, :], share[:, 0, :], group_mass[:], ALU.mult))
                    link(V.reciprocal(weight[:, :, 0], share[:, 1, :]))
                    link(V.tensor_tensor(weight[:, :, 1], weight[:, :, 0], gap[:], ALU.mult))
                    dve.wait_ge(rank_ready, 1)
                    link(V.memset(before[:, 0], 0.0))
                    for t in range(NT):
                        link(V.tensor_tensor(before[:, t + 1], before[:, t], count_ps[:, t], ALU.add))
                    link(V.tensor_tensor(ranks[:], rank_ps, before[:, 0:NT], ALU.add))
                    counts = before[:, NT]
                    link(V.tensor_scalar(extra_of[:], counts, float(SLOTS), None, ALU.is_gt))
                    for j in range(2, (n_tok - 1) // SLOTS + 1):
                        link(V.scalar_tensor_tensor(extra_of[:], counts, float(SLOTS * j), extra_of[:], ALU.is_gt, ALU.add))
                    link(V.tensor_tensor_scan(blocks_after[:], P.ones[:, 0:N_EXPERTS], extra_of[:], 0.0, ALU.mult, ALU.add))
                    link(V.tensor_tensor(blocks_before[:], blocks_after[:], extra_of[:], ALU.subtract))
                    link(V.tensor_copy(n_extra[:], blocks_after[:, N_EXPERTS - 1:N_EXPERTS]))
                    link(V.tensor_tensor(ended[:], count[:, 0:EXTRA].unsqueeze(2).to_broadcast([PART, EXTRA, N_EXPERTS]),
                                         blocks_after[:].unsqueeze(1).to_broadcast([PART, EXTRA, N_EXPERTS]), ALU.is_ge))
                    link(V.tensor_reduce(extra_f[:], ended[:], AX.X, ALU.add))
                    link(V.tensor_scalar(extra_expert[:], extra_f[:], float(N_EXPERTS - 1), None, ALU.min))
                    for j in range(2):
                        link(V.tensor_tensor(work[:], chosen[:, j], ranks[:], ALU.mult))
                        link(V.tensor_reduce(rank[:, j, :], work[:], AX.X, ALU.add))
                        link(V.tensor_scalar(turn[:, j, :], rank[:, j, :], float(SLOTS), None, ALU.is_ge))
                        for m in range(2, (n_tok - 1) // SLOTS + 1):
                            link(V.scalar_tensor_tensor(turn[:, j, :], rank[:, j, :], float(SLOTS * m), turn[:, j, :], ALU.is_ge, ALU.add))
                        link(V.scalar_tensor_tensor(place[:, j, :], turn[:, j, :], -float(SLOTS), rank[:, j, :], ALU.mult, ALU.add))
                        link(V.tensor_tensor(work[:], chosen[:, j], blocks_before[:].unsqueeze(1).to_broadcast([PART, NT, N_EXPERTS]), ALU.mult))
                        link(V.tensor_reduce(block_of[:, j, :], work[:], AX.X, ALU.add))
                        link(V.scalar_tensor_tensor(block_of[:, j, :], block_of[:, j, :], float(N_EXPERTS - 1), turn[:, j, :], ALU.add, ALU.add))
                        link(V.tensor_tensor(block_of[:, j, :], block_of[:, j, :], index[:, j, :], ALU.subtract))
                        link(V.tensor_scalar(more[:, j, :], turn[:, j, :], 0.0, None, ALU.is_gt))
                        link(V.tensor_tensor(more[:, j, :], more[:, j, :], block_of[:, j, :], ALU.mult))
                        link(V.tensor_tensor(block_of[:, j, :], more[:, j, :], index[:, j, :], ALU.add))
                        link(V.scalar_tensor_tensor(row_of[:, :, j], block_of[:, j, :], float(SLOTS), place[:, j, :], ALU.mult, ALU.add))
                        dve.sem_inc(placed, 1)
                        for t in range(NT):
                            V.tensor_scalar(slot_hot[:, j, t, :], count[:, 0:SLOTS], place[:, j, t:t + 1], None, ALU.is_equal).then_inc(hot_ready, 1)
                    dve.wait_ge(slots_ready, 1)
                    V.tensor_copy(slot_token[:], slot_ps).then_inc(slots_taken, 1)
                    dve.wait_ge(slots_taken, 1)

        def blocks_run():
            with ExitStack() as ctx:
                sb, ps, sem = scope(nc, ctx, tag + "b")
                rows_in = [sb(f"rows_in{s}", [SLOTS, D]) for s in range(2)]
                token_now = [sb(f"token_now{s}", [SLOTS, 1], I32) for s in range(2)]
                feats = [sb(f"feats{s}", [PART, DC, SLOTS]) for s in range(2)]
                silu = [sb(f"silu{s}", [PART, EC, SLOTS]) for s in range(2)]
                hidden = [sb(f"hidden{s}", [PART, EC, SLOTS]) for s in range(2)]
                result = [sb(f"result{s}", [SLOTS, D]) for s in range(2)]
                HALF = DC // 2
                turned_lo, turned_hi = (ps(n, [PART, HALF, PART])[:, :, 0:SLOTS] for n in ("turned_lo", "turned_hi"))
                gate_ps = [ps(f"gate_ps{s}", [PART, EC, PART])[:, :, 0:SLOTS] for s in range(2)]
                up_ps = [ps(f"up_ps{s}", [PART, EC, PART])[:, :, 0:SLOTS] for s in range(2)]
                result_ps = ps("result_ps", [SLOTS, D])
                index_ready, index_seen = sem("index_ready"), sem("index_seen")
                gathered = [P.pool_sems[l][s] for s in range(2)]
                stored = [sem(f"stored{s}") for s in range(2)]
                turned_ready, feats_act, feats_dve = sem("turned_ready"), sem("feats_act"), sem("feats_dve")
                wide_done, silu_ready, hidden_ready, result_ready = sem("wide_done"), sem("silu_ready"), sem("hidden_ready"), sem("result_ready")
                result_act, result_dve = sem("result_act"), sem("result_dve")
                PAIRS = N_EXPERTS // 2

                def turn_rows(s):
                    by_chunk = rows_in[s][:].rearrange("t (p c) -> t c p", c=DC)
                    for c in range(DC):
                        last = nc.tensor.transpose((turned_lo, turned_hi)[c // HALF][:, c % HALF, :], by_chunk[:, c, :], P.ident[0:SLOTS, 0:SLOTS])
                    return last

                def wide_products(s):
                    for acc, w in ((gate_ps, w_gate), (up_ps, w_up)):
                        for f in range(EC):
                            for c in range(DC):
                                last = nc.tensor.matmul(acc[s][:, f, :], w[s][:, c, f * PART:(f + 1) * PART], feats[s][:, c, :],
                                                        start=c == 0, stop=c == DC - 1)
                    return last

                def down_products(s):
                    for half in range(2):
                        for f in range(EC):
                            last = nc.tensor.matmul(result_ps[:, half * BANK:(half + 1) * BANK], hidden[s][:, f, :],
                                                    w_down[s][:, f, half * BANK:(half + 1) * BANK], start=f == 0, stop=f == EC - 1)
                    return last

                with ExitStack() as main:
                    block = main.enter_context(nc.Block())

                    @block.sync
                    def _(sp):
                        with sp.Fori(1, PAIRS) as i:
                            for s in range(2):
                                sp.wait_ge(wide_done, i * 2 + s - 1)
                                expert_weights(sp, s, bass.ds(i * 2 + s, 1))
                                sp.wait_ge(result_ready, i * 2 + s - 1)
                                sp.dma_start(w_down[s][:], A["moe_w_down"][l, bass.ds(i * 2 + s, 1)].rearrange(
                                    "a (c p) n -> p (a c) n", p=PART)).then_inc(down_in[s], 16)

                    @block.gpsimd
                    def _(pool):
                        for s in range(2):
                            nc.gpsimd.tensor_copy(token_now[s][:], slot_token[:, s:s + 1]).then_inc(index_ready, 1)
                            pool.wait_ge(index_ready, s + 1)
                            nc.gpsimd.indirect_dma_start(rows_in[s][:], None, P.h_dram[0:n_tok, :],
                                                         bass.IndirectOffsetOnAxis(ap=token_now[s][:], axis=0)).then_inc(gathered[s], 16)
                        with pool.Fori(0, PAIRS) as i:
                            for s in range(2):
                                pool.wait_ge(turned_ready, i * 2 + s + 1)
                                nc.gpsimd.tensor_copy(token_now[s][:], slot_token[:, bass.ds(i * 2 + s + 2, 1)]).then_inc(index_ready, 1)
                                pool.wait_ge(index_ready, i * 2 + s + 3)
                                pool.sem_inc(index_seen, 1)
                                nc.gpsimd.indirect_dma_start(rows_in[s][:], None, P.h_dram[0:n_tok, :],
                                                             bass.IndirectOffsetOnAxis(ap=token_now[s][:], axis=0)).then_inc(gathered[s], 16)
                        for s in range(2):
                            pool.wait_ge(gathered[s], PAIRS * 16 + 16)

                    @block.tensor
                    def _(pe):
                        pe.wait_ge(gathered[0], 16)
                        turn_rows(0).then_inc(turned_ready, 1)
                        with pe.Fori(0, PAIRS) as i:
                            for s in range(2):
                                e = i * 2 + s
                                pe.wait_ge(feats_act, e + 1)
                                pe.wait_ge(feats_dve, e + 1)
                                pe.wait_ge(wide_in[s], i * 32 + 32)
                                wide_products(s).then_inc(wide_done, 1)
                                pe.wait_ge(gathered[1 - s], i * 16 + 16 * (s + 1))
                                turn_rows(1 - s).then_inc(turned_ready, 1)
                                pe.wait_ge(down_in[s], i * 16 + 16)
                                pe.wait_ge(hidden_ready, e + 1)
                                pe.wait_ge(result_act, e + 1)
                                pe.wait_ge(result_dve, e + 1)
                                down_products(s).then_inc(result_ready, 1)

                    @block.scalar
                    def _(act):
                        act.sem_inc(result_act, 1)
                        for s in range(2):
                            act.sem_inc(stored[s], 16)
                        act.wait_ge(turned_ready, 1)
                        nc.scalar.activation(feats[0][:, 0:HALF, :], turned_lo, ACT.Copy).then_inc(feats_act, 1)
                        with act.Fori(0, PAIRS) as i:
                            for s in range(2):
                                e = i * 2 + s
                                act.wait_ge(wide_done, e + 1)
                                nc.scalar.activation(silu[s][:], gate_ps[s], ACT.Silu).then_inc(silu_ready, 1)
                                act.wait_ge(turned_ready, e + 2)
                                nc.scalar.activation(feats[1 - s][:, 0:HALF, :], turned_lo, ACT.Copy).then_inc(feats_act, 1)
                                act.wait_ge(result_ready, e + 1)
                                act.wait_ge(stored[s], i * 16 + 16)
                                nc.scalar.activation(result[s][:, 0:BANK], result_ps[:, 0:BANK], ACT.Copy).then_inc(result_act, 1)
                                act.wait_ge(result_act, e + 2)
                                act.wait_ge(result_dve, e + 2)
                                act.dma_start(P.y_dram[bass.ds(e * SLOTS, SLOTS), :], result[s][:]).then_inc(stored[s], 16)
                        for s in range(2):
                            act.wait_ge(stored[s], PAIRS * 16 + 16)

                    @block.vector
                    def _(dve):
                        dve.sem_inc(result_dve, 1)
                        dve.wait_ge(turned_ready, 1)
                        nc.vector.tensor_copy(feats[0][:, HALF:DC, :], turned_hi).then_inc(feats_dve, 1)
                        with dve.Fori(0, PAIRS) as i:
                            for s in range(2):
                                e = i * 2 + s
                                dve.wait_ge(silu_ready, e + 1)
                                nc.vector.tensor_tensor(hidden[s][:], silu[s][:], up_ps[s], ALU.mult).then_inc(hidden_ready, 1)
                                dve.wait_ge(turned_ready, e + 2)
                                nc.vector.tensor_copy(feats[1 - s][:, HALF:DC, :], turned_hi).then_inc(feats_dve, 1)
                                dve.wait_ge(result_ready, e + 1)
                                dve.wait_ge(stored[s], i * 16 + 16)
                                nc.vector.tensor_copy(result[s][:, BANK:D], result_ps[:, BANK:D]).then_inc(result_dve, 1)

                with ExitStack() as extra:
                    sb, ps, sem = scope(nc, extra, tag + "x")
                    x_weights, x_stored, x_done = sem("weights"), sem("stored"), sem("done")
                    x_gathered = P.pool_sems[l][2]
                    x_index, x_turned, x_act, x_dve = sem("index"), sem("turned"), sem("act"), sem("dve")
                    x_wide, x_silu, x_hidden, x_result = sem("wide"), sem("silu"), sem("hidden"), sem("result")
                    block = extra.enter_context(nc.Block())

                    @block.sync
                    def _(sp):
                        n = nc.sync.value_load(n_extra[0:1, 0:1], min_val=0, max_val=EXTRA)
                        with sp.Fori(0, EXTRA) as i:
                            with sp.If(n > i):
                                e = nc.sync.value_load(extra_expert[0:1, bass.ds(i, 1)], min_val=0, max_val=N_EXPERTS - 1)
                                for w, src, form in ((w_gate, "moe_w_gate", "a (p c) n -> p (a c) n"), (w_up, "moe_w_up", "a (p c) n -> p (a c) n")):
                                    sp.dma_start(w[0][:], A[src][l, bass.ds(e, 1)].rearrange(form, c=DC)).then_inc(x_weights, 16)
                                sp.dma_start(w_down[0][:], A["moe_w_down"][l, bass.ds(e, 1)].rearrange("a (c p) n -> p (a c) n", p=PART)).then_inc(x_weights, 16)
                                sp.wait_ge(x_act, i * 2 + 2)
                                sp.wait_ge(x_dve, i * 2 + 2)
                                sp.dma_start(P.y_dram[bass.ds((i + N_EXPERTS) * SLOTS, SLOTS), :], result[0][:]).then_inc(x_stored, 16)
                                sp.wait_ge(x_stored, i * 16 + 16)
                                sp.sem_inc(x_done, 1)

                    @block.gpsimd
                    def _(pool):
                        pool.sem_inc(x_done, 1)
                        n = nc.gpsimd.value_load(n_extra[0:1, 0:1], min_val=0, max_val=EXTRA)
                        with pool.Fori(0, EXTRA) as i:
                            with pool.If(n > i):
                                pool.wait_ge(x_done, i + 1)
                                nc.gpsimd.tensor_copy(token_now[0][:], slot_token[:, bass.ds(i + N_EXPERTS, 1)]).then_inc(x_index, 1)
                                pool.wait_ge(x_index, i + 1)
                                pool.sem_inc(index_seen, 1)
                                nc.gpsimd.indirect_dma_start(rows_in[0][:], None, P.h_dram[0:n_tok, :],
                                                             bass.IndirectOffsetOnAxis(ap=token_now[0][:], axis=0)).then_inc(x_gathered, 16)

                    @block.tensor
                    def _(pe):
                        n = nc.tensor.value_load(n_extra[0:1, 0:1], min_val=0, max_val=EXTRA)
                        with pe.Fori(0, EXTRA) as i:
                            with pe.If(n > i):
                                pe.wait_ge(x_gathered, i * 16 + 16)
                                turn_rows(0).then_inc(x_turned, 1)
                                pe.wait_ge(x_weights, i * 48 + 48)
                                pe.wait_ge(x_act, i * 2 + 1)
                                pe.wait_ge(x_dve, i * 2 + 1)
                                wide_products(0).then_inc(x_wide, 1)
                                pe.wait_ge(x_hidden, i + 1)
                                down_products(0).then_inc(x_result, 1)

                    @block.scalar
                    def _(act):
                        n = nc.scalar.value_load(n_extra[0:1, 0:1], min_val=0, max_val=EXTRA)
                        with act.Fori(0, EXTRA) as i:
                            with act.If(n > i):
                                act.wait_ge(x_turned, i + 1)
                                nc.scalar.activation(feats[0][:, 0:HALF, :], turned_lo, ACT.Copy).then_inc(x_act, 1)
                                act.wait_ge(x_wide, i + 1)
                                nc.scalar.activation(silu[0][:], gate_ps[0], ACT.Silu).then_inc(x_silu, 1)
                                act.wait_ge(x_result, i + 1)
                                nc.scalar.activation(result[0][:, 0:BANK], result_ps[:, 0:BANK], ACT.Copy).then_inc(x_act, 1)

                    @block.vector
                    def _(dve):
                        n = nc.vector.value_load(n_extra[0:1, 0:1], min_val=0, max_val=EXTRA)
                        with dve.Fori(0, EXTRA) as i:
                            with dve.If(n > i):
                                dve.wait_ge(x_turned, i + 1)
                                nc.vector.tensor_copy(feats[0][:, HALF:DC, :], turned_hi).then_inc(x_dve, 1)
                                dve.wait_ge(x_silu, i + 1)
                                nc.vector.tensor_tensor(hidden[0][:], silu[0][:], up_ps[0], ALU.mult).then_inc(x_hidden, 1)
                                dve.wait_ge(x_result, i + 1)
                                nc.vector.tensor_copy(result[0][:, BANK:D], result_ps[:, BANK:D]).then_inc(x_dve, 1)

        def combine():
            with ExitStack() as ctx:
                sb, ps, sem = scope(nc, ctx, tag + "c")
                picked = [[sb(f"picked{n}{j}", [PART, D]) for j in range(2)] for n in range(2)]
                mixed = [sb(f"mixed{n}", [PART, D]) for n in range(2)]
                row_now = sb("row_now", [PART, NT, 2, 1], I32)
                turned = [ps(f"turned{n}", [PART, DC, PART]) for n in range(2)]
                picked_in = [P.pool_sems[l][3 + n] for n in range(2)]
                halved, mixed_ready, turned_ready, added = sem("halved"), sem("mixed_ready"), sem("turned_ready"), sem("added")
                block = ctx.enter_context(nc.Block())

                @block.gpsimd
                def _(pool):
                    for t in range(NT):
                        if t >= 2:
                            pool.wait_ge(mixed_ready, t - 1)
                        for j in range(2):
                            nc.gpsimd.indirect_dma_start(picked[t % 2][j][:], None, P.y_dram[0:BLOCKS * SLOTS, :],
                                                         bass.IndirectOffsetOnAxis(ap=row_of[:, t, j:j + 1], axis=0)).then_inc(picked_in[t % 2], 16)

                @block.tensor
                def _(pe):
                    for t in range(NT):
                        pe.wait_ge(mixed_ready, t + 1)
                        if t >= 2:
                            pe.wait_ge(added, (t - 1) * DC)
                        for c in range(DC):
                            last = nc.tensor.transpose(turned[t % 2][:, c, :], mixed[t % 2][:, c * PART:(c + 1) * PART], P.ident[:])
                        last.then_inc(turned_ready, 1)

                @block.vector
                def _(dve):
                    def mix(t):
                        dve.wait_ge(picked_in[t % 2], 32 * (t // 2 + 1))
                        if t >= 2:
                            dve.wait_ge(turned_ready, t - 1)
                        nc.vector.tensor_scalar(mixed[t % 2][:], picked[t % 2][0][:], weight[:, t, 0:1], None, ALU.mult).then_inc(halved, 1)
                        dve.wait_ge(halved, t + 1)
                        nc.vector.scalar_tensor_tensor(mixed[t % 2][:], picked[t % 2][1][:], weight[:, t, 1:2], mixed[t % 2][:],
                                                       ALU.mult, ALU.add).then_inc(mixed_ready, 1)

                    mix(0)
                    for t in range(NT):
                        if t + 1 < NT:
                            mix(t + 1)
                        dve.wait_ge(turned_ready, t + 1)
                        at = first_tok + t * PART
                        w = int(at < CTX)
                        for c in range(DC):
                            x = P.x[:, c, at:at + PART]
                            nc.vector.scalar_tensor_tensor(x, turned[t % 2][:, c, :], P.mod[:, l, 5 * DC + c, w:w + 1], x,
                                                           ALU.mult, ALU.add).then_inc(added, 1)

        route()
        blocks_run()
        combine()


def clear_rows(P, sp):
    cols = P.zero.shape[-1]
    zero = P.zero[0:SLOTS].unsqueeze(1).to_broadcast([SLOTS, D // cols, cols])
    for b in range(N_EXPERTS, BLOCKS_MAX):
        sp.dma_start(P.y_dram[b * SLOTS:(b + 1) * SLOTS, :].rearrange("p (a b) -> p a b", b=cols), zero).then_inc(P.rows_cleared, 16)


CLEARED = 16 * (BLOCKS_MAX - N_EXPERTS)


def window_tables(nc, A, K, P, tag, rpb_cols, heads, table):
    H = heads.stop - heads.start
    J = REL_R - 1
    PER = 4
    with ExitStack() as ctx:
        sb, ps, sem = scope(nc, ctx, tag)
        band, outside = sb("band", [BAND_ROWS, 3 * GRID_W - 1]), sb("outside", [PART, GRID_W])
        picked = [ps(f"picked{n}", [PART, BANK]) for n in range(2)]
        consts_in, picked_ready, taken = sem("consts_in"), sem("picked_ready"), sem("taken")
        block = ctx.enter_context(nc.Block())

        def view(n):
            return picked[n % 2][:, 0:PER * H * J].rearrange("p (c h j) -> p c h j", c=PER, h=H)

        @block.sync
        def _(sp):
            sp.dma_start(band[:], K["band"]).then_inc(consts_in, 16)
            sp.dma_start(outside[:], K["outside"]).then_inc(consts_in, 16)

        @block.tensor
        def _(pe):
            pe.wait_ge(consts_in, 32)
            for n in range(GRID_W // PER):
                if n >= 2:
                    pe.wait_ge(taken, n - 1)
                for c in range(PER):
                    at = GRID_W - 1 - (n * PER + c)
                    last = nc.tensor.matmul(view(n)[:, c], band[:, at:at + PART], rpb_cols[:, heads, :], start=True, stop=True)
                last.then_inc(picked_ready, 1)

        @block.vector
        def _(dve):
            dve.wait_ge(consts_in, 32)
            for n in range(GRID_W // PER):
                dve.wait_ge(picked_ready, n + 1)
                cols = slice(n * PER, (n + 1) * PER)
                nc.vector.tensor_tensor(table[:, cols].rearrange("p c h j -> p c (h j)"), view(n).rearrange("p c h j -> p c (h j)"),
                                        outside[:, cols].unsqueeze(2).to_broadcast([PART, PER, H * J]), ALU.add).then_inc(taken, 1)


def neighbourhood_mixer(nc, A, K, P, q, first, ahead):
    with ExitStack() as ctx:
        sb, _, _ = scope(nc, ctx, "na")
        k = sb("k", [PART, DC, TOK])
        v = P.h[:].rearrange("p a b -> p (a b)").rearrange("p (t d) -> p t d", t=TOK_T)
        products = []
        for n in range(3 * D // HALF_SLAB):
            part, at = divmod(n, D // HALF_SLAB)
            if part == 0:
                for j in range(2):
                    products.append(SplitProduct(
                        n, lambda w, x, j=j: [(w[:, c, j * PART:(j + 1) * PART], x[:, c, LAT]) for c in range(DC)], (PART, SEQ),
                        copy_to(nc, q[:, 2 * at + j, :], HEAD ** -0.5)))
            elif part == 1:
                feature_slab(nc, products, n, lambda j, at=at: k[:, 2 * at + j, :], wide(TOK))
            else:
                token_slab(nc, products, n, lambda t, at=at: v[:, t, at * HALF_SLAB:(at + 1) * HALF_SLAB], TOK_T)
        split_stage(nc, P, "na_in", P.h, half_slabs(P, A["na_w_in"][0]), products, first)
        rpb_cols = sb("rpb_cols", [BAND_ROWS, H_C, REL_R - 1])
        with ExitStack() as low:
            sb, ps, sem = scope(nc, low, "rpb")
            ROWS_IN = H_C * REL_R // 2
            raw = sb("raw", [ROWS_IN, 2, REL_C])
            turned = [ps(f"turned{odd}", [PART, BANK]) for odd in range(2)]
            raw_in, cleared, turned_ready, taken = sem("raw_in"), sem("cleared"), sem("turned_ready"), sem("taken")
            block = low.enter_context(nc.Block())

            @block.sync
            def _(sp):
                sp.dma_start(raw[:], A["na_rpb"][0].rearrange("(n h) r c -> (h r) n c", n=2)).then_inc(raw_in, 16)

            @block.tensor
            def _(pe):
                pe.wait_ge(raw_in, 16)
                for odd in range(2):
                    for n in range(2):
                        last = nc.tensor.matmul(turned[odd][odd * GRID_W:odd * GRID_W + REL_C, n * ROWS_IN:(n + 1) * ROWS_IN], raw[:, n, :],
                                                P.ident[0:ROWS_IN, 0:ROWS_IN], start=True, stop=True)
                    last.then_inc(turned_ready, 1)

            @block.vector
            def _(dve):
                nc.vector.memset(rpb_cols[:], 0.0).then_inc(cleared, 1)
                dve.wait_ge(cleared, 1)
                for odd in range(2):
                    dve.wait_ge(turned_ready, odd + 1)
                    rows = slice(odd * GRID_W, odd * GRID_W + REL_C)
                    nc.vector.tensor_copy(rpb_cols[rows], turned[odd][rows, 0:2 * ROWS_IN].rearrange("p (h r) -> p h r", r=REL_R)[:, :, 1 - odd:REL_R - odd]
                                          ).then_inc(taken, 1)

        groups = [QueryGroup(tiles=[(t * PART, TOK) for t in range(SEQ_T)], first=lambda c: 0)]
        HALF = H_C // 2
        for part in range(2):
            with ExitStack() as low:
                sb, _, _ = scope(nc, low, f"win{part}")
                table = sb("table", [PART, GRID_W, HALF, REL_R - 1])
                window_tables(nc, A, K, P, f"tab{part}", rpb_cols, slice(part * HALF, (part + 1) * HALF), table)
                pair0 = part * HALF // 2

                def source(i, s):
                    return (q[s * HEAD:(s + 1) * HEAD, bass.ds(i + pair0, 1), :],
                            v[:, :, bass.ds((i + pair0) * 2 * HEAD + s * HEAD, HEAD)])

                def keys(i, s):
                    return k[:, bass.ds(i + pair0, 1), :]

                def out(i, s, q0, n):
                    return q[s * HEAD:(s + 1) * HEAD, bass.ds(i + pair0, 1), q0:q0 + n]

                def bias(i, s, t):
                    j0 = REL_R // 2 - 1 - 2 * t
                    rows = table[:, :, bass.ds(i * 2 + s, 1), j0:j0 + ROWS].rearrange("p c a r -> p (a r) c")
                    return [(0, CTX, None), (CTX, SEQ, rows)]

                attention_stage(nc, P, f"attn_n{part}", [HeadPairs(PART, True, HALF // 2, source, keys, out, bias)], groups, TOK,
                                ahead if part == 1 else None)


def lat_norm_job(P, gain, bias):
    return [NormJob(n=SEQ, src=[P.x[:, c, LAT] for c in range(DC)], dst=[P.x[:, c, LAT] for c in range(DC)],
                            gain=[gain(c) for c in range(DC)], bias=None if bias is None else [bias(c) for c in range(DC)],
                    sums=P.ones, size=D)]


def final_norm(nc, P, ahead):
    at = P.col["norm_final"]
    norm_stage(nc, P, "final", lat_norm_job(P, lambda c: P.cols[:, at + c:at + c + 1], None), 0, ahead=ahead)


def layer_norm(nc, P, l, which, ahead):
    g, b = (P.col[n] + (2 * l + which) * DC for n in ("ln_g_2", "ln_b_2"))
    norm_stage(nc, P, f"ln{l}{which}", lat_norm_job(P, lambda c: P.cols[:, g + c:g + c + 1], lambda c: P.cols[:, b + c:b + c + 1]),
               1, center=True, ahead=ahead)


def retention_stage(nc, K, P, q, k, v, y):
    with ExitStack() as ctx:
        sb, ps, sem = scope(nc, ctx, "ret")
        decay = sb("decay", [PART, RET_H, SEQ])
        weighted = [sb(f"weighted{n}", [PART, SEQ]) for n in range(2)]
        scores = [ps(f"scores{n}", [PART, BANK]) for n in range(2)]
        acc = [ps(f"acc{n}", [PART, BANK]) for n in range(2)]
        decay_in, scores_ready, weighted_ready, acc_ready, taken = (
            sem(n) for n in ("decay_in", "scores_ready", "weighted_ready", "acc_ready", "taken"))
        block = ctx.enter_context(nc.Block())
        N = RET_H * SEQ_T

        @block.sync
        def _(sp):
            sp.dma_start(decay[:], K["decay"]).then_inc(decay_in, 16)

        @block.tensor
        def _(pe):
            def score(n):
                h, b = divmod(n, SEQ_T)
                if n >= 2:
                    pe.wait_ge(weighted_ready, n - 1)
                nc.tensor.matmul(scores[n % 2][:, b * PART:], k[:, h, b * PART:(b + 1) * PART], q[:, h, b * PART:],
                                 start=True, stop=True).then_inc(scores_ready, 1)

            score(0)
            for n in range(N):
                h, b = divmod(n, SEQ_T)
                if n + 1 < N:
                    score(n + 1)
                pe.wait_ge(weighted_ready, n + 1)
                if h >= 2 and b == 0:
                    pe.wait_ge(taken, h - 1)
                last = nc.tensor.matmul(acc[h % 2][:, b * PART:], v[:, b, h * RET_D:(h + 1) * RET_D], weighted[n % 2][:, b * PART:],
                                        start=b == 0, stop=b == SEQ_T - 1)
                last.then_inc(acc_ready, 1)

        @block.vector
        def _(dve):
            dve.wait_ge(decay_in, 16)
            for n in range(N):
                h, b = divmod(n, SEQ_T)
                dve.wait_ge(scores_ready, n + 1)
                if n >= 2:
                    dve.wait_ge(acc_ready, n - 1)
                nc.vector.tensor_tensor(weighted[n % 2][:, b * PART:], scores[n % 2][:, b * PART:], decay[:, h, 0:SEQ - b * PART],
                                        ALU.mult).then_inc(weighted_ready, 1)

        @block.scalar
        def _(act):
            for h in range(RET_H):
                act.wait_ge(acc_ready, (h + 1) * SEQ_T)
                nc.scalar.activation(y[:, h, :], acc[h % 2][:], ACT.Copy).then_inc(taken, 1)


def distance_tables(nc, A, K, P, table):
    SPAN = SEQ + PART
    with ExitStack() as ctx:
        sb, ps, sem = scope(nc, ctx, "dist")
        by_bucket, seen = sb("by_bucket", [PART, SPAN]), sb("seen", [PART, SEQ])
        bias, bias_wide = sb("bias", [PART, DSA_H]), sb("bias_wide", [PART, DSA_H, PART])
        rows = [sb(f"rows{n}", [PART, SPAN]) for n in range(2)]
        acc = [ps(f"acc{n}", [PART, 2, BANK]) for n in range(2)]
        ins, widened, acc_ready, rows_ready, added = (sem(n) for n in ("ins", "widened", "acc_ready", "rows_ready", "added"))
        out = [sem(f"out{n}") for n in range(2)]
        back, cleared = sem("back"), sem("cleared")
        block = ctx.enter_context(nc.Block())
        parts = ((0, 0, BANK), (1, BANK, SPAN))

        @block.sync
        def _(sp):
            sp.wait_ge(cleared, 1)
            sp.dma_start(bias[0:T5_BUCKETS, :], A["rel_bias_2"]).then_inc(ins, 16)
            sp.dma_start(by_bucket[:], K["by_bucket"]).then_inc(ins, 16)
            sp.dma_start(seen[:], K["seen"]).then_inc(ins, 16)
            for h in range(DSA_H):
                sp.wait_ge(rows_ready, h + 1)
                sp.dma_start(P.t_dram[h].rearrange("(p y) -> p y", p=PART), rows[h % 2][:]).then_inc(out[h % 2], 16)
            for h in range(DSA_H):
                sp.wait_ge(out[h % 2], 16 * (h // 2 + 1))
            for h in range(DSA_H):
                shifted = P.t_dram[h, PART - 1:PART - 1 + PART * (SPAN - 1)].rearrange("(p y) -> p y", p=PART)
                sp.dma_start(table[:, h, :], shifted[:, 0:SEQ]).then_inc(back, 16)

        @block.tensor
        def _(pe):
            pe.wait_ge(widened, 1)
            for h in range(DSA_H):
                if h >= 2:
                    pe.wait_ge(rows_ready, h - 1)
                for b, a, e in parts:
                    last = nc.tensor.matmul(acc[h % 2][:, b, 0:e - a], bias_wide[:, h, :], by_bucket[:, a:e], start=True, stop=True)
                last.then_inc(acc_ready, 1)

        @block.vector
        def _(dve):
            nc.vector.memset(bias[:], 0.0).then_inc(cleared, 1)
            dve.wait_ge(ins, 48)
            nc.vector.tensor_copy(bias_wide[:], bias[:].unsqueeze(2).to_broadcast([PART, DSA_H, PART])).then_inc(widened, 1)
            for h in range(DSA_H):
                dve.wait_ge(acc_ready, h + 1)
                if h >= 2:
                    dve.wait_ge(out[h % 2], 16 * (h // 2))
                nc.vector.tensor_copy(rows[h % 2][:], acc[h % 2][:].rearrange("p b n -> p (b n)")[:, 0:SPAN]).then_inc(rows_ready, 1)
            dve.wait_ge(back, 16 * DSA_H)
            nc.vector.tensor_tensor(table[:], table[:], seen[:].unsqueeze(1).to_broadcast([PART, DSA_H, SEQ]), ALU.add).then_inc(added, 1)


def even_mixer(nc, A, K, P, first, ahead):
    with ExitStack() as ctx:
        sb, _, _ = scope(nc, ctx, "even")
        qk = sb("qk", [PART, 2 * RET_H, SEQ])
        v = sb("v", [PART, SEQ_T, RET_H * RET_D])
        g = sb("g", [PART, RET_H, SEQ])
        qkd = sb("qkd", [PART, DSA_H, SEQ])
        vd = sb("vd", [PART, SEQ_T, DSA_H * HEAD])
        products, whole = [], [slice(0, SEQ)]
        PER = RET_H * RET_D // HALF_SLAB
        for n in range(7 * PER):
            part, at = divmod(n, PER)
            if part in (2, 6):
                token_slab(nc, products, n, lambda t, d=v if part == 2 else vd, at=at: d[:, t, at * HALF_SLAB:(at + 1) * HALF_SLAB], SEQ_T)
            else:
                d, j0, scale = {0: (qk, 0, None), 1: (qk, RET_H, RET_D ** -0.5), 3: (g, 0, None), 4: (qkd, 0, HEAD ** -0.5),
                                5: (qkd, DSA_H // 2, None)}[part]
                feature_slab(nc, products, n, lambda j, d=d, at=j0 + 2 * at: d[:, at + j, :], whole, scale, ACT.Silu if part == 3 else None)
        split_stage(nc, P, "even_in", P.x[:, :, LAT], half_slabs(P, A["even_w_in_2"][0]), products, first)
        rope_stage(nc, P, "rotary", K, [(qk[:, c, :], 0, PART, "r") for c in range(2 * RET_H)])
        with ExitStack() as low:
            sb, _, _ = scope(nc, low, "even_y")
            y = sb("y", [PART, RET_H, SEQ])
            retention_stage(nc, K, P, qk[:, 0:RET_H, :], qk[:, RET_H:, :], v, y)
            jobs = [NormJob(n=SEQ, src=[y[:, h, :]], dst=[y[:, h, :]], gain=[P.ones[:, 0:1]], bias=None, sums=P.ones, size=RET_D,
                            gated=([g[:, h, :]], [P.o[:, h, LAT]])) for h in range(RET_H)]
            norm_stage(nc, P, "head_norm", jobs, 1, center=True)
        with ExitStack() as low:
            sb, _, _ = scope(nc, low, "even_d")
            table = sb("table", [PART, DSA_H, SEQ])
            distance_tables(nc, A, K, P, table)
            groups = [QueryGroup(tiles=[(t * PART, (t + 1) * PART) for t in range(SEQ_T)], first=lambda c: c)]

            def source(i, s):
                return qkd[s * HEAD:(s + 1) * HEAD, bass.ds(i, 1), :], vd[:, :, bass.ds(i * 2 * HEAD + s * HEAD, HEAD)]

            def keys(i, s):
                return qkd[:, bass.ds(i + DSA_H // 2, 1), :]

            def out(i, s, q0, n):
                return P.o[s * HEAD:(s + 1) * HEAD, bass.ds(i + RET_H, 1), CTX + q0:CTX + q0 + n]

            def bias(i, s, t):
                return [(0, (t + 1) * PART, table[:, bass.ds(i * 2 + s, 1), SEQ - (t + 1) * PART:SEQ])]

            attention_stage(nc, P, "attn_d", [HeadPairs(PART, True, DSA_H // 2, source, keys, out, bias)], groups, SEQ, ahead)


def convolved(nc, P, c, n_chunks, y):
    def tap(back):
        at = P.col["odd_conv_w_2"] + (ML_CONV - 1 - back) * n_chunks + c
        return P.cols[:, at:at + 1]

    def take(engine, result, link):
        ins = nc.vector.tensor_scalar(y, result, tap(0), None, ALU.mult)
        for back in range(1, ML_CONV):
            link(ins)
            ins = nc.vector.scalar_tensor_tensor(y[:, back:], result[:, 0:SEQ - back], tap(back), y[:, back:], ALU.mult, ALU.add)
        return ins
    return take


def memory_gates(nc, A, K, P, raw_i, raw_f, key_log, minus_top, floor):
    with ExitStack() as ctx:
        sb, ps, sem = scope(nc, ctx, "gates")
        bias_i, bias_f = sb("bias_i", [ML_H, 1]), sb("bias_f", [ML_H, 1])
        row = sb("row", [ML_H, ML_H, PART])
        log_f, minus, low, tail, run, u, g, f_g = (sb(n, [ML_H, SEQ]) for n in ("log_f", "minus", "low", "tail", "run", "u", "g", "f_g"))
        ones = sb("ones", [ML_H, SEQ])
        spread = [ps(f"spread{n}", [PART, BANK]) for n in range(4)]
        turned = ps("turned", [PART, SEQ_T, ML_H])
        ins, step, tail_ready, tail_done, gates_ready = (sem(n) for n in ("ins", "step", "tail_ready", "tail_done", "gates_ready"))
        turned_ready, spread_ready, taken_top, taken_floor, taken_u = (
            sem(n) for n in ("turned_ready", "spread_ready", "taken_top", "taken_floor", "taken_u"))
        block = ctx.enter_context(nc.Block())

        @block.sync
        def _(sp):
            sp.dma_start(bias_i[:], A["odd_gate_b_2"][0, 0:ML_H].rearrange("(p a) -> p a", a=1)).then_inc(ins, 16)
            sp.dma_start(bias_f[:], A["odd_gate_b_2"][0, ML_H:].rearrange("(p a) -> p a", a=1)).then_inc(ins, 16)
            sp.dma_start(row[:], K["row"]).then_inc(ins, 16)

        @block.vector
        def _(dve):
            link = Link(dve, step)
            V = nc.vector
            link(V.memset(ones[:], 1.0))
            dve.wait_ge(ins, 48)
            link(V.tensor_scalar(log_f[:], raw_f[:], bias_f[:], None, ALU.add))
            link(V.tensor_scalar(minus[:], log_f[:], -1.0, None, ALU.mult))
            V.tensor_tensor(tail[:], log_f[:], minus[:], ALU.min).then_inc(tail_ready, 1)
            link(V.tensor_scalar(low[:], log_f[:], 0.0, None, ALU.min))
            dve.wait_ge(tail_done, 2)
            link(V.tensor_tensor(log_f[:], low[:], tail[:], ALU.subtract))
            link(V.tensor_tensor_scan(run[:], ones[:], log_f[:], 0.0, ALU.mult, ALU.add))
            link(V.scalar_tensor_tensor(u[:], raw_i[:], bias_i[:], run[:], ALU.add, ALU.subtract))
            link(V.tensor_tensor_scan(g[:], ones[:], u[:], 0.0, ALU.mult, ALU.max))
            link(V.tensor_scalar(g[:], g[:], -1.0, None, ALU.mult))
            V.tensor_tensor(f_g[:], g[:], run[:], ALU.subtract).then_inc(gates_ready, 1)
            dve.wait_ge(turned_ready, 1)
            V.tensor_copy(key_log[:], turned[:]).then_inc(taken_u, 1)
            for h in range(ML_H):
                dve.wait_ge(spread_ready, 2 * h + 1)
                V.tensor_copy(minus_top[:, h, :], spread[2 * h % 4][:]).then_inc(taken_top, 1)

        @block.scalar
        def _(act):
            act.wait_ge(tail_ready, 1)
            nc.scalar.activation(tail[:], tail[:], ACT.Exp).then_inc(tail_done, 1)
            act.wait_ge(tail_done, 1)
            nc.scalar.activation(tail[:], tail[:], ACT.Ln, bias=ones[:, 0:1]).then_inc(tail_done, 1)
            for h in range(ML_H):
                act.wait_ge(spread_ready, 2 * h + 2)
                nc.scalar.activation(floor[:, h, :], spread[(2 * h + 1) % 4][:], ACT.Exp).then_inc(taken_floor, 1)

        @block.tensor
        def _(pe):
            pe.wait_ge(ins, 48)
            pe.wait_ge(gates_ready, 1)
            for t in range(SEQ_T):
                last = nc.tensor.transpose(turned[:, t, :], u[:, t * PART:(t + 1) * PART], P.ident[0:ML_H, 0:ML_H])
            last.then_inc(turned_ready, 1)
            for h in range(ML_H):
                if h >= 2:
                    pe.wait_ge(taken_top, h - 1)
                    pe.wait_ge(taken_floor, h - 1)
                nc.tensor.matmul(spread[2 * h % 4][:], row[:, h, :], g[:], start=True, stop=True).then_inc(spread_ready, 1)
                nc.tensor.matmul(spread[(2 * h + 1) % 4][:], row[:, h, :], f_g[:], start=True, stop=True).then_inc(spread_ready, 1)


def memory_stage(nc, K, P, q, k, v, gate_o, key_log, minus_top, floor, ahead):
    DCH = ML_D // PART
    with ExitStack() as ctx:
        sb, ps, sem = scope(nc, ctx, "mem")
        future = sb("future", [PART, PART])
        masked = [sb(f"masked{n}", [PART, PART]) for n in range(2)]
        decay = [sb(f"decay{n}", [PART, SEQ]) for n in range(2)]
        weighted = [sb(f"weighted{n}", [PART, SEQ]) for n in range(2)]
        size = sb("size", [PART, SEQ])
        part = [sb(f"part{n}", [PART, SEQ]) for n in range(DCH)]
        scores = [ps(f"scores{n}", [PART, BANK]) for n in range(2)]
        acc = [[ps(f"acc{n}{e}", [PART, BANK]) for e in range(DCH + 1)] for n in range(2)]
        future_in, masked_ready, decay_ready, scores_ready = sem("future_in"), sem("masked_ready"), sem("decay_ready"), sem("scores_ready")
        weighted_ready, acc_ready, step, done = sem("weighted_ready"), sem("acc_ready"), sem("step"), sem("done")
        block = ctx.enter_context(nc.Block())
        N = ML_H * SEQ_T

        @block.sync
        def _(sp):
            sp.dma_start(future[:], K["future"]).then_inc(future_in, 16)
            ahead.start(sp)

        @block.tensor
        def _(pe):
            def score(n):
                h, b = divmod(n, SEQ_T)
                if n >= 2:
                    pe.wait_ge(weighted_ready, n - 1)
                for c in range(DCH):
                    last = nc.tensor.matmul(scores[n % 2][:, b * PART:], k[:, h * DCH + c, b * PART:(b + 1) * PART],
                                            q[:, h * DCH + c, b * PART:], start=c == 0, stop=c == DCH - 1)
                last.then_inc(scores_ready, 1)

            score(0)
            for n in range(N):
                h, b = divmod(n, SEQ_T)
                if n + 1 < N:
                    score(n + 1)
                pe.wait_ge(weighted_ready, n + 1)
                if h >= 2 and b == 0:
                    pe.wait_ge(done, (h - 1) * DCH)
                for e in range(DCH + 1):
                    lhs_t = v[:, b, h * ML_D + e * PART:h * ML_D + (e + 1) * PART] if e < DCH else P.ones[:]
                    last = nc.tensor.matmul(acc[h % 2][e][:, b * PART:], lhs_t, weighted[n % 2][:, b * PART:],
                                            start=b == 0, stop=b == SEQ_T - 1)
                last.then_inc(acc_ready, 1)

        @block.scalar
        def _(act):
            for n in range(N):
                h, b = divmod(n, SEQ_T)
                if n >= 2:
                    act.wait_ge(weighted_ready, n - 1)
                act.wait_ge(masked_ready, n + 1)
                u = key_log[:, b, h:h + 1]
                nc.scalar.activation(decay[n % 2][:, b * PART:(b + 1) * PART], masked[n % 2][:], ACT.Exp, bias=u).then_inc(decay_ready, 1)
                if b < SEQ_T - 1:
                    nc.scalar.activation(decay[n % 2][:, (b + 1) * PART:], minus_top[:, h, (b + 1) * PART:], ACT.Exp, bias=u).then_inc(decay_ready, 1)

        @block.vector
        def _(dve):
            link = Link(dve, step)
            V = nc.vector
            dve.wait_ge(future_in, 16)

            def mask(n):
                h, b = divmod(n, SEQ_T)
                V.tensor_tensor(masked[n % 2][:], minus_top[:, h, b * PART:(b + 1) * PART], future[:], ALU.add).then_inc(masked_ready, 1)

            mask(0)
            mask(1)
            per_head = 2 * SEQ_T - 1
            for n in range(N):
                h, b = divmod(n, SEQ_T)
                dve.wait_ge(decay_ready, h * per_head + min(2 * b + 2, per_head))
                dve.wait_ge(scores_ready, n + 1)
                if n >= 2:
                    dve.wait_ge(acc_ready, n - 1)
                V.scalar_tensor_tensor(weighted[n % 2][:, b * PART:], scores[n % 2][:, b * PART:], ML_D ** -0.5, decay[n % 2][:, b * PART:],
                                       ALU.mult, ALU.mult).then_inc(weighted_ready, 1)
                if n + 2 < N:
                    mask(n + 2)
                if b == SEQ_T - 1:
                    dve.wait_ge(acc_ready, n + 1)
                    link(V.scalar_tensor_tensor(size[:], acc[h % 2][DCH][:], -1.0, floor[:, h, :], ALU.mult, ALU.max))
                    link(V.tensor_tensor(size[:], size[:], acc[h % 2][DCH][:], ALU.max))
                    link(V.reciprocal(size[:], size[:]))
                    for e in range(DCH):
                        link(V.tensor_tensor(part[e][:], acc[h % 2][e][:], size[:], ALU.mult))
                        V.tensor_tensor(P.o[:, h * DCH + e, LAT], part[e][:], gate_o[:, h * DCH + e, :], ALU.mult).then_inc(done, 1)


def odd_mixer(nc, A, K, P, first, ahead):
    with ExitStack() as ctx:
        sb, _, _ = scope(nc, ctx, "odd")
        QK = 2 * ML_H * ML_D // PART
        qk = sb("qk", [PART, QK, SEQ])
        v = sb("v", [PART, SEQ_T, ML_H * ML_D])
        o = sb("o", [PART, ML_H * ML_D // PART, SEQ])
        raw_i, raw_f = sb("raw_i", [ML_H, SEQ]), sb("raw_f", [ML_H, SEQ])
        w, WIDE = A["odd_w_in_2"][0], 4 * ML_H * ML_D
        products, whole = [], [slice(0, SEQ)]
        for n in range(WIDE // HALF_SLAB):
            part, at = divmod(n, ML_H * ML_D // HALF_SLAB)
            if part < 2:
                for j in range(2):
                    c = 2 * n + j
                    products.append(SplitProduct(
                        n, lambda w, x, j=j: [(w[:, k, j * PART:(j + 1) * PART], x[:, k, :]) for k in range(DC)], (PART, SEQ),
                        convolved(nc, P, c, QK, qk[:, c, :]), "dve", lambda c=c: nc.scalar.activation(qk[:, c, :], qk[:, c, :], ACT.Silu)))
            elif part == 2:
                token_slab(nc, products, n, lambda t, at=at: v[:, t, at * HALF_SLAB:(at + 1) * HALF_SLAB], SEQ_T)
            else:
                feature_slab(nc, products, n, lambda j, at=2 * at: o[:, at + j, :], whole, func=ACT.Sigmoid)
        split_stage(nc, P, "odd_in", P.x[:, :, LAT], half_slabs(P, w[:, 0:WIDE]), products, first)
        with ExitStack() as low:
            sb2, _, _ = scope(nc, low, "odd_gates")
            gates_w = sb2("gates_w", [PART, DC, 2 * ML_H])
            products = [product([(gates_w[:, c, j * ML_H:(j + 1) * ML_H], P.x[:, c, LAT]) for c in range(DC)], (0, ML_H, SEQ), copy_to(nc, dst[:]))
                        for j, dst in enumerate((raw_i, raw_f))]
            product_stage(nc, P, "odd_gates", [load(gates_w[:], rows_of(w)[:, :, WIDE:])], products)
        key_log = sb("key_log", [PART, SEQ_T, ML_H])
        minus_top, floor = sb("minus_top", [PART, ML_H, SEQ]), sb("floor", [PART, ML_H, SEQ])
        memory_gates(nc, A, K, P, raw_i, raw_f, key_log, minus_top, floor)
        memory_stage(nc, K, P, qk[:, 0:QK // 2, :], qk[:, QK // 2:, :], v, o, key_log, minus_top, floor, ahead)


def up_pieces(A, P, l, s, j):
    w = rows_of(A["ffn_w_up_2"][l])
    slot = P.ahead[:].rearrange("p (s n a) (b m) -> p s n (a b) m", s=2, n=2, m=PART)
    return [(slot[:, s, n], w[:, :, bass.ds(j * PART + n * D_FF, PART)]) for n in range(2)]


def ffn_stage(nc, A, P, l, first):
    tag = f"ffn{l}"
    PAIRS = FC // 2
    RING = 4
    with ExitStack() as ctx:
        sb, _, sem = scope(nc, ctx, tag)
        hidden = sb("hidden", [PART, FC, SEQ])
        down = [sb(f"down{s}", [PART, D]) for s in range(RING)]
        ends = sb("ends", [PART, 2, D])
        ends_in = sem("ends_in")
        down_in = [sem(f"down_in{s}") for s in range(RING)]
        w_down = A["ffn_w_down_2"][l]
        with ExitStack() as up:
            sb, ps, sem = scope(nc, up, tag + "u")
            raw = P.ahead[:].rearrange("p (s n a) (b m) -> p s (n a b m)", s=2, n=2, m=PART)
            w_hi, w_lo = ([sb(f"w_{part}{s}", [PART, 2, DC, PART], F32R) for s in range(2)] for part in ("hi", "lo"))
            x_hi, x_lo = (sb(f"x_{part}", [PART, DC, SEQ], F32R) for part in ("hi", "lo"))
            mixed = [sb(f"mixed{s}", [PART, SEQ]) for s in range(2)]
            gate_ps = [ps(f"gate_ps{s}", [PART, BANK]) for s in range(2)]
            up_ps = [ps(f"up_ps{s}", [PART, BANK]) for s in range(2)]
            slab_in = [sem(f"slab_in{s}") for s in range(2)]
            acc_ready, conv_step, silu_ready, hidden_ready = sem("acc_ready"), sem("conv_step"), sem("silu_ready"), sem("hidden_ready")
            w_rounded, w_split, x_rounded, x_split = sem("w_rounded"), sem("w_split"), sem("x_rounded"), sem("x_split")
            block = up.enter_context(nc.Block())
            taps, shift = P.col[f"ffn_conv_w_2:{l}"], P.col["ffn_conv_b_2"] + l * FC

            @block.sync
            def _(sp):
                first.wait(sp)
                for s in range(2):
                    sp.sem_inc(slab_in[s], 32)
                with sp.Fori(1, PAIRS) as i:
                    for s in range(2):
                        sp.wait_ge(w_split, i * 2 + s - 1)
                        for slot, source in up_pieces(A, P, l, s, i * 2 + s):
                            sp.dma_start(slot, source).then_inc(slab_in[s], 16)
                for n, at in enumerate((0, (FC - 1) * PART)):
                    sp.dma_start(ends[:, n, :], w_down[at:at + PART, :]).then_inc(ends_in, 16)
                for s in range(RING):
                    sp.dma_start(down[s][:], w_down[(1 + s) * PART:(2 + s) * PART, :]).then_inc(down_in[s], 16)

            @block.tensor
            def _(pe):
                for c in range(DC):
                    pe.wait_ge(x_split, c + 1)
                with pe.Fori(0, PAIRS) as i:
                    for s in range(2):
                        pe.wait_ge(w_split, i * 2 + s + 1)
                        pe.wait_ge(hidden_ready, i * 2 + s + 1)
                        for n, acc in enumerate((gate_ps, up_ps)):
                            operands = split_products([(w_hi[s][:, n, c, :], w_lo[s][:, n, c, :], x_hi[:, c, :], x_lo[:, c, :]) for c in range(DC)])
                            for k, (lhs_t, rhs) in enumerate(operands):
                                last = nc.tensor.matmul(acc[s][:], lhs_t, rhs, start=k == 0, stop=k == len(operands) - 1)
                        last.then_inc(acc_ready, 1)

            @block.vector
            def _(dve):
                V = nc.vector
                dve.sem_inc(hidden_ready, 2)

                def split(s, j, arrivals):
                    hi, lo = (w[s][:].rearrange("p n c m -> p (n c m)") for w in (w_hi, w_lo))
                    dve.wait_ge(slab_in[s], arrivals)
                    V.tensor_copy(hi, raw[:, s]).then_inc(w_rounded, 1)
                    dve.wait_ge(w_rounded, j + 1)
                    V.tensor_tensor(lo, raw[:, s], hi.bitcast(F32), ALU.subtract).then_inc(w_split, 1)

                def process(s, i):
                    j = i * 2 + s

                    def col(at):
                        return P.cols[:, bass.ds(j + at, 1)]

                    dve.wait_ge(acc_ready, j + 1)
                    V.tensor_scalar(mixed[s][:], gate_ps[s][:], col(taps + (FFN_CONV - 1) * FC), col(shift), ALU.mult, ALU.add).then_inc(conv_step, 1)
                    for back in range(1, FFN_CONV):
                        dve.wait_ge(conv_step, i * 2 * FFN_CONV + s * FFN_CONV + back)
                        V.scalar_tensor_tensor(mixed[s][:, back:], gate_ps[s][:, 0:SEQ - back], col(taps + (FFN_CONV - 1 - back) * FC),
                                               mixed[s][:, back:], ALU.mult, ALU.add).then_inc(conv_step, 1)
                    dve.wait_ge(silu_ready, j + 1)
                    V.tensor_tensor(hidden[:, bass.ds(j, 1), :], mixed[s][:].unsqueeze(1), up_ps[s][:].unsqueeze(1), ALU.mult).then_inc(hidden_ready, 1)

                split(0, 0, 32)
                for c in range(DC):
                    V.tensor_copy(x_hi[:, c, :], P.x[:, c, LAT]).then_inc(x_rounded, 1)
                for c in range(DC):
                    dve.wait_ge(x_rounded, c + 1)
                    V.tensor_tensor(x_lo[:, c, :], P.x[:, c, LAT], x_hi[:, c, :].bitcast(F32), ALU.subtract).then_inc(x_split, 1)
                with dve.Fori(0, PAIRS - 1) as i:
                    split(1, i * 2 + 1, i * 32 + 32)
                    process(0, i)
                    split(0, i * 2 + 2, i * 32 + 64)
                    process(1, i)
                split(1, FC - 1, PAIRS * 32)
                process(0, PAIRS - 1)
                process(1, PAIRS - 1)

            @block.scalar
            def _(act):
                with act.Fori(0, PAIRS) as i:
                    for s in range(2):
                        act.wait_ge(conv_step, i * 2 * FFN_CONV + (s + 1) * FFN_CONV)
                        nc.scalar.activation(mixed[s][:], mixed[s][:], ACT.Silu).then_inc(silu_ready, 1)

        with ExitStack() as last:
            sb, ps, sem = scope(nc, last, tag + "d")
            TURNS = (FC - 2) // RING
            acc = [ps(f"acc{c}", [PART, BANK]) for c in range(DC)]
            w_hi, w_lo = ([sb(f"w_{part}{s}", [PART, D], F32R) for s in range(2)] for part in ("hi", "lo"))
            h_hi, h_lo = ([sb(f"h_{part}{s}", [PART, SEQ], F32R) for s in range(2)] for part in ("hi", "lo"))
            rounded, split_done, acc_step, taken = sem("rounded"), sem("split_done"), sem("acc_step"), sem("taken")
            block = last.enter_context(nc.Block())

            @block.sync
            def _(sp):
                with sp.Fori(1, TURNS) as i:
                    for s in range(RING):
                        sp.wait_ge(split_done, (i * RING + s + 2 - RING) * 2)
                        sp.dma_start(down[s][:], w_down[bass.ds((i * RING + s + 1) * PART, PART), :]).then_inc(down_in[s], 16)

            @block.tensor
            def _(pe):
                pe.sem_inc(acc_step, 2)

                def chunk(slot, j, start=False, stop=False):
                    pe.wait_ge(split_done, j * 2 + 2)
                    for c in range(DC):
                        m = slice(c * PART, (c + 1) * PART)
                        operands = split_products([(w_hi[slot][:, m], w_lo[slot][:, m], h_hi[slot][:], h_lo[slot][:])])
                        for k, (lhs_t, rhs) in enumerate(operands):
                            ins = nc.tensor.matmul(acc[c][:], lhs_t, rhs, start=start and k == 0, stop=stop and k == len(operands) - 1)
                    ins.then_inc(acc_step, 1)

                chunk(0, 0, start=True)
                with pe.Fori(0, TURNS) as i:
                    for s in range(RING):
                        chunk((s + 1) % 2, i * RING + s + 1)
                chunk((FC - 1) % 2, FC - 1, stop=True)

            @block.vector
            def _(dve):
                V = nc.vector

                def split(slot, j, weights, rows):
                    dve.wait_ge(acc_step, j + 1)
                    V.tensor_copy(w_hi[slot][:], weights).then_inc(rounded, 1)
                    V.tensor_copy(h_hi[slot][:].unsqueeze(1), rows).then_inc(rounded, 1)
                    dve.wait_ge(rounded, j * 2 + 2)
                    V.tensor_tensor(w_lo[slot][:], weights, w_hi[slot][:].bitcast(F32), ALU.subtract).then_inc(split_done, 1)
                    V.tensor_tensor(h_lo[slot][:].unsqueeze(1), rows, h_hi[slot][:].bitcast(F32).unsqueeze(1), ALU.subtract).then_inc(split_done, 1)

                dve.wait_ge(ends_in, 32)
                split(0, 0, ends[:, 0, :], hidden[:, 0:1, :])
                with dve.Fori(0, TURNS) as i:
                    for s in range(RING):
                        j = i * RING + s + 1
                        dve.wait_ge(down_in[s], i * 16 + 16)
                        split((s + 1) % 2, j, down[s][:], hidden[:, bass.ds(j, 1), :])
                split((FC - 1) % 2, FC - 1, ends[:, 1, :], hidden[:, FC - 1:FC, :])
                dve.wait_ge(acc_step, FC + 2)
                for c in range(DC):
                    x = P.x[:, c, LAT]
                    V.scalar_tensor_tensor(x, x, ALPHA, acc[c][:], ALU.mult, ALU.add).then_inc(taken, 1)


def store_stage(nc, P, out):
    with ExitStack() as ctx:
        sb, ps, sem = scope(nc, ctx, "store")
        rows = [sb(f"rows{n}", [PART, D]) for n in range(2)]
        turned = [[ps(f"turned{n}{half}", [PART, BANK]) for half in range(2)] for n in range(2)]
        turned_ready, act_done, dve_done = sem("turned_ready"), sem("act_done"), sem("dve_done")
        stored = [sem(f"stored{n}") for n in range(2)]
        block = ctx.enter_context(nc.Block())

        @block.tensor
        def _(pe):
            for t in range(SEQ_T):
                if t >= 2:
                    pe.wait_ge(act_done, t - 1)
                    pe.wait_ge(dve_done, t - 1)
                for c in range(DC):
                    half, at = divmod(c * PART, BANK)
                    last = nc.tensor.transpose(turned[t % 2][half][:, at:at + PART], P.x[:, c, CTX + t * PART:CTX + (t + 1) * PART], P.ident[:])
                last.then_inc(turned_ready, 1)

        @block.scalar
        def _(act):
            for t in range(SEQ_T):
                act.wait_ge(turned_ready, t + 1)
                if t >= 2:
                    act.wait_ge(stored[t % 2], 16 * (t // 2))
                nc.scalar.activation(rows[t % 2][:, 0:BANK], turned[t % 2][0][:], ACT.Copy).then_inc(act_done, 1)

        @block.vector
        def _(dve):
            for t in range(SEQ_T):
                dve.wait_ge(turned_ready, t + 1)
                if t >= 2:
                    dve.wait_ge(stored[t % 2], 16 * (t // 2))
                nc.vector.tensor_copy(rows[t % 2][:, BANK:], turned[t % 2][1][:]).then_inc(dve_done, 1)

        @block.sync
        def _(sp):
            for t in range(SEQ_T):
                sp.wait_ge(act_done, t + 1)
                sp.wait_ge(dve_done, t + 1)
                sp.dma_start(out[0, t * PART:(t + 1) * PART, :], rows[t % 2][:]).then_inc(stored[t % 2], 16)
            for n in range(2):
                sp.wait_ge(stored[n], 16 * (SEQ_T // 2))


class Place:

    def __init__(self, col):
        self.col = col


def build(nc, A, K, out):
    with ExitStack() as ctx:
        sb, _, _ = scope(nc, ctx, "all")
        P = Place(col=param_columns())
        P.x = sb("x", [PART, DC, TOK])
        P.h = sb("h", [PART, DC, TOK])
        P.cols = sb("cols", [PART, len(PARAM_BLOCKS) * PART])
        P.cond = sb("cond", [PART, DC, 2])
        P.mod = sb("mod", [PART, DEPTH, 6 * DC, 2])
        P.scale = sb("scale", [PART, DEPTH, 2, DC, 2])
        P.gq_gain = sb("gq_gain", [PART, 1])
        P.eps = sb("eps", [PART, 2])
        P.ident, P.ones, P.half_ones = (sb(n, [PART, PART]) for n in ("ident", "ones", "half_ones"))
        P.ahead = sb("ahead", [PART, DC, BANK])
        P.ahead_in, P.ahead_loads = nc.alloc_semaphore("ahead_in"), 0
        P.zero, P.rows_cleared = sb("zero", [PART, 128]), nc.alloc_semaphore("rows_cleared")
        P.h_dram = nc.dram_tensor("h_rows", [TOK, D], F32, kind="Internal").ap()
        P.t_dram = nc.dram_tensor("t_rows", [DSA_H, PART * (SEQ + PART)], F32, kind="Internal").ap()
        P.y_dram = nc.dram_tensor("y_rows", [BLOCKS_MAX * SLOTS, D], F32, kind="Internal").ap()
        P.pool_sems = [[nc.alloc_semaphore(f"pool{l}_{n}") for n in range(5)] for l in range(DEPTH)]
        both = [(slice(0, CTX), 1), (LAT, 0)]
        def ahead(slabs):
            return Ahead(P, slabs[0] + slabs[1])

        def gated(l, at):
            def take(j, t):
                w = int(at + t.start < CTX)
                return add_scaled(nc, P.x[:, j, at + t.start:at + t.stop], P.mod[:, l, 2 * DC + j, w:w + 1])
            return take

        whole = [slice(0, SEQ)]
        load_stage(nc, A, K, P)
        conditioning_stage(nc, A, P)
        coming = Ahead(P, [(P.ahead[:], rows_of(A["ab_w_in"][0])[:, :, 0:BANK])])
        norm_stage(nc, P, "mod0", modulate_jobs(P, 0, 0, both), 0, ahead=coming)
        slabs = ab_out_slabs(P, A["ab_w_out"][0])
        first, coming = coming, ahead(slabs)
        latent_mixer(nc, A, K, P, first, coming)
        out_stage(nc, P, "ab_out", slabs, P.o, wide(TOK), gated(0, 0), coming)
        norm_stage(nc, P, "ffn0", modulate_jobs(P, 0, 1, both), 0)
        expert_stage(nc, A, K, P, 0, 0)
        coming = ahead(half_slabs(P, A["na_w_in"][0]))
        norm_stage(nc, P, "mod1", modulate_jobs(P, 1, 0, both), 0, ahead=coming)
        with ExitStack() as layer:
            sb, _, _ = scope(nc, layer, "na")
            q = sb("q", [PART, DC, SEQ])
            slabs = half_slabs(P, A["na_w_out"][0])
            first, coming = coming, ahead(slabs)
            neighbourhood_mixer(nc, A, K, P, q, first, coming)
            out_stage(nc, P, "na_out", slabs, q, whole, gated(1, CTX), coming)
        norm_stage(nc, P, "ffn1", modulate_jobs(P, 1, 1, both[1:]), 0)
        expert_stage(nc, A, K, P, 1, CTX)
        P.o = P.h
        mixers = ((even_mixer, A["even_w_in_2"][0], A["even_w_out_2"][0]), (odd_mixer, A["odd_w_in_2"][0], A["odd_w_out_2"][0]))
        coming = ahead(half_slabs(P, mixers[0][1]))
        final_norm(nc, P, coming)
        for l, (mixer, w_in, w_out) in enumerate(mixers):
            slabs = half_slabs(P, w_out)
            first, coming = coming, ahead(slabs)
            mixer(nc, A, K, P, first, coming)
            out_stage(nc, P, f"deep_out{l}", slabs, P.o[:, :, LAT], whole, lambda j, t: add_deep(nc, P.x[:, j, LAT]), coming)
            coming = Ahead(P, up_pieces(A, P, l, 0, 0) + up_pieces(A, P, l, 1, 1))
            layer_norm(nc, P, l, 0, coming)
            ffn_stage(nc, A, P, l, coming)
            coming = ahead(half_slabs(P, mixers[l + 1][1])) if l + 1 < DEPTH else None
            layer_norm(nc, P, l, 1, coming)
        store_stage(nc, P, out)


_OUT = ((1, SEQ, D), "float32")


def kernel(**inputs):
    import concourse.bacc as bacc
    from concourse.bass_utils import run_bass_kernel_spmd

    nc = bacc.Bacc("TRN2", target_bir_lowering=False, num_devices=1)
    arrays, A, K = {}, {}, {}
    for kind, group, place in (("in", inputs, A), ("const", shape_constants(), K)):
        for name, value in group.items():
            a = np.ascontiguousarray(value)
            arrays[f"{kind}_{name}"] = a
            place[name] = nc.dram_tensor(f"{kind}_{name}", a.shape, mybir.dt.from_np(a.dtype), kind="ExternalInput").ap()
    out = nc.dram_tensor("out", _OUT[0], F32, kind="ExternalOutput").ap()
    build(nc, A, K, out)
    result = run_bass_kernel_spmd(nc, [arrays], core_ids=[0])
    return result.results[0]["out"]
```
